# Optimizing a Trainium2 kernel written in Bass

```python
import math
import jax, jax.numpy as jnp
from jax import lax
import numpy as np

D_MODEL = 1024
BATCH = 1
SEQ = 256
DEPTH = 2
DEC_BATCH = 8
DEC_SEQ = 8
PAST_LEN = 2048
PAGE_SIZE = 128

N_MIXERS = 2
N_HGRN_LAYERS = (DEPTH + 1) // 2
N_SSM_LAYERS = DEPTH // 2
HGRN_EXPAND = 128
HGRN_HEADS = D_MODEL // HGRN_EXPAND
HGRN_DK = HGRN_EXPAND
HGRN_DV = D_MODEL // HGRN_HEADS
HGRN_FD = HGRN_HEADS * HGRN_DK
HGRN_ID = HGRN_HEADS * HGRN_DV
HGRN_CHUNK = 64
SSM_GROUP = 16
SSM_GROUPS = D_MODEL // SSM_GROUP
SSM_STATE = 64
D_FF = 2816
N_EXPERTS = 8
TOP_K = 2
D_FF_EXPERT = 2816
NORM_EPS = 1e-6

kernel_name = 'hgrn2_s5_hybrid_decoder_step'

def _rmsnorm(x, w):
    xf = x.astype(jnp.float32)
    y = xf * lax.rsqrt(jnp.mean(xf * xf, axis=-1, keepdims=True) + NORM_EPS)
    return (y * w.astype(jnp.float32)).astype(x.dtype)

def _modulation(c, w, b):
    m = jax.nn.silu(c) @ w + b
    return jnp.split(m[:, None, :], 6, axis=-1)

def _swiglu(h, w_in, w_out):
    g, u = jnp.split(h @ w_in, 2, axis=-1)
    return (jax.nn.silu(g) * u) @ w_out

def _moe_swiglu(h, w_router, b_router, w_in, w_out):
    logits = h.astype(jnp.float32) @ w_router.astype(jnp.float32) + b_router.astype(jnp.float32)
    vals, idx = lax.top_k(logits, TOP_K)
    probs = jax.nn.softmax(vals, axis=-1)
    gates = jnp.sum(jax.nn.one_hot(idx, N_EXPERTS, dtype=jnp.float32) * probs[..., None], axis=-2)
    out = jnp.zeros(h.shape, jnp.float32)
    for e in range(N_EXPERTS):
        out = out + gates[..., e:e + 1] * _swiglu(h, w_in[e], w_out[e]).astype(jnp.float32)
    return out.astype(h.dtype)

def _hgrn2_lower_bounds(lb_param):
    p = jax.nn.softmax(lb_param.astype(jnp.float32), axis=0)
    cs = jnp.cumsum(p, axis=0)
    return cs - cs[0:1]

def _gla_chunk_scan(q, k, v, logf, s0):
    bsz, seqlen, nh, dk = q.shape
    dv = v.shape[-1]
    csz = math.gcd(seqlen, HGRN_CHUNK)
    nch = seqlen // csz

    def to_chunks(t):
        return t.reshape(bsz, nch, csz, nh, t.shape[-1]).transpose(1, 0, 3, 2, 4)

    causal = jnp.tril(jnp.ones((csz, csz), dtype=bool))[:, :, None]

    def step(state, inp):
        qi, ki, vi, gi = inp
        b = jnp.cumsum(gi, axis=2)
        o_inter = jnp.einsum('bhtd,bhde->bhte', qi * jnp.exp(b), state)
        diff = b[:, :, :, None, :] - b[:, :, None, :, :]
        decay = jnp.exp(jnp.where(causal, diff, -jnp.inf))
        scores = jnp.einsum('bhtd,bhsd,bhtsd->bhts', qi, ki, decay)
        o = o_inter + jnp.einsum('bhts,bhse->bhte', scores, vi)
        b_last = b[:, :, -1:, :]
        new_state = (jnp.exp(b_last[:, :, 0, :])[..., None] * state
                     + jnp.einsum('bhsd,bhse->bhde', ki * jnp.exp(b_last - b), vi))
        return new_state, o

    s_fin, o = lax.scan(step, s0, (to_chunks(q), to_chunks(k), to_chunks(v), to_chunks(logf)))
    o = o.transpose(1, 0, 3, 2, 4).reshape(bsz, seqlen, nh, dv)
    return o, s_fin

def _hgrn2_mixer(h, s0, w_in, lb, gnorm_w, w_out):
    bsz, seqlen, _ = h.shape
    q, f, i, g = jnp.split(h @ w_in, [HGRN_FD, 2 * HGRN_FD, 2 * HGRN_FD + HGRN_ID], axis=-1)
    q = jax.nn.silu(q.astype(jnp.float32))
    logf = jnp.logaddexp(jnp.log(lb), jnp.log1p(-lb) + jax.nn.log_sigmoid(f.astype(jnp.float32)))
    k = -jnp.expm1(logf)

    def heads(t, d):
        return t.reshape(bsz, seqlen, HGRN_HEADS, d)

    o, s_new = _gla_chunk_scan(heads(q, HGRN_DK), heads(k, HGRN_DK), heads(i.astype(jnp.float32), HGRN_DV),
                               heads(logf, HGRN_DK), s0.astype(jnp.float32))
    o = _rmsnorm(o, gnorm_w) * jax.nn.silu(heads(g.astype(jnp.float32), HGRN_DV))
    return o.reshape(bsz, seqlen, HGRN_ID).astype(h.dtype) @ w_out, s_new

def _complex_affine_combine(e1, e2):
    a1r, a1i, b1r, b1i = e1
    a2r, a2i, b2r, b2i = e2
    return (a2r * a1r - a2i * a1i,
            a2r * a1i + a2i * a1r,
            a2r * b1r - a2i * b1i + b2r,
            a2r * b1i + a2i * b1r + b2i)

def _s5_mixer(h, x0_re, x0_im, a_re, a_im, log_dt, b_re, b_im, c_re, c_im, d_skip, w_glu):
    bsz, seqlen, _ = h.shape
    a_re, a_im, b_re, b_im, c_re, c_im = (t.astype(jnp.float32) for t in (a_re, a_im, b_re, b_im, c_re, c_im))
    u = h.astype(jnp.float32).reshape(bsz, seqlen, SSM_GROUPS, SSM_GROUP)
    dt = jnp.exp(log_dt.astype(jnp.float32))[:, None]
    mag = jnp.exp(a_re * dt)
    lam_re = mag * jnp.cos(a_im * dt)
    lam_im = mag * jnp.sin(a_im * dt)
    den = a_re * a_re + a_im * a_im
    coef_re = ((lam_re - 1.0) * a_re + lam_im * a_im) / den
    coef_im = (lam_im * a_re - (lam_re - 1.0) * a_im) / den
    bb_re = coef_re[..., None] * b_re - coef_im[..., None] * b_im
    bb_im = coef_re[..., None] * b_im + coef_im[..., None] * b_re
    bu_re = jnp.einsum('gpc,blgc->lbgp', bb_re, u)
    bu_im = jnp.einsum('gpc,blgc->lbgp', bb_im, u)
    x0_re = x0_re.astype(jnp.float32)
    x0_im = x0_im.astype(jnp.float32)
    bu_re = bu_re.at[0].add(lam_re * x0_re - lam_im * x0_im)
    bu_im = bu_im.at[0].add(lam_re * x0_im + lam_im * x0_re)
    shape_a = (seqlen, 1, SSM_GROUPS, SSM_STATE)
    lam_re_t = jnp.broadcast_to(lam_re, shape_a)
    lam_im_t = jnp.broadcast_to(lam_im, shape_a)
    _, _, xs_re, xs_im = lax.associative_scan(_complex_affine_combine, (lam_re_t, lam_im_t, bu_re, bu_im), axis=0)
    y = jnp.einsum('gcp,lbgp->blgc', c_re, xs_re) - jnp.einsum('gcp,lbgp->blgc', c_im, xs_im)
    y = (y + d_skip.astype(jnp.float32).reshape(SSM_GROUPS, SSM_GROUP) * u).reshape(bsz, seqlen, D_MODEL)
    z = jax.nn.gelu(y).astype(h.dtype)
    za, zb = jnp.split(z @ w_glu, 2, axis=-1)
    return za * jax.nn.sigmoid(zb), xs_re[-1], xs_im[-1]

def _trunk(x, c, s_hgrn, s_re, s_im, norm_w, ada_w, ada_b, hgrn_w_in, hgrn_lb, hgrn_gnorm, hgrn_w_out,
           ssm_a_re, ssm_a_im, ssm_log_dt, ssm_b_re, ssm_b_im, ssm_c_re, ssm_c_im, ssm_d, ssm_w_glu,
           ffn_w_in, ffn_w_out, moe_w_router, moe_b_router, moe_w_in, moe_w_out, final_norm_w):
    lower_bounds = _hgrn2_lower_bounds(hgrn_lb)
    new_hgrn, new_re, new_im = [], [], []
    for layer in range(DEPTH):
        slot = layer // N_MIXERS
        sh1, sc1, g1, sh2, sc2, g2 = _modulation(c, ada_w[layer], ada_b[layer])
        h = _rmsnorm(x, norm_w[layer, 0]) * (1.0 + sc1) + sh1
        if layer % N_MIXERS == 0:
            m, s_new = _hgrn2_mixer(h, s_hgrn[slot], hgrn_w_in[slot], lower_bounds[slot],
                                    hgrn_gnorm[slot], hgrn_w_out[slot])
            new_hgrn.append(s_new)
        else:
            m, xr, xi = _s5_mixer(h, s_re[slot], s_im[slot], ssm_a_re[slot], ssm_a_im[slot], ssm_log_dt[slot],
                                  ssm_b_re[slot], ssm_b_im[slot], ssm_c_re[slot], ssm_c_im[slot],
                                  ssm_d[slot], ssm_w_glu[slot])
            new_re.append(xr)
            new_im.append(xi)
        x = x + g1 * m
        h = _rmsnorm(x, norm_w[layer, 1]) * (1.0 + sc2) + sh2
        if layer % 2 == 0:
            f = _swiglu(h, ffn_w_in[slot], ffn_w_out[slot])
        else:
            f = _moe_swiglu(h, moe_w_router[slot], moe_b_router[slot], moe_w_in[slot], moe_w_out[slot])
        x = x + g2 * f
    return _rmsnorm(x, final_norm_w), jnp.stack(new_hgrn), jnp.stack(new_re), jnp.stack(new_im)

def setup_inputs(seed: int = 0) -> dict:
    key = jax.random.key(seed)
    ks = jax.random.split(key, 32)

    def nrm(k, shape, s):
        return jax.random.normal(k, shape, jnp.float32) * s

    D = D_MODEL
    g, p, sg = SSM_GROUPS, SSM_STATE, SSM_GROUP
    n_dense = N_HGRN_LAYERS
    n_moe = N_SSM_LAYERS
    return {
        'x_prompt': nrm(ks[0], (BATCH, SEQ, D), 1.0),
        'x_sample': nrm(ks[1], (DEC_BATCH, DEC_SEQ, D), 1.0),
        'state_hgrn': nrm(ks[2], (N_HGRN_LAYERS, DEC_BATCH, HGRN_HEADS, HGRN_DK, HGRN_DV), 0.5),
        'state_ssm_re': nrm(ks[3], (N_SSM_LAYERS, DEC_BATCH, g, p), 0.5),
        'state_ssm_im': nrm(ks[4], (N_SSM_LAYERS, DEC_BATCH, g, p), 0.5),
        'c_prompt': nrm(ks[5], (BATCH, D), 1.0),
        'c_sample': nrm(ks[6], (DEC_BATCH, D), 1.0),
        'norm_w': 1.0 + nrm(ks[7], (DEPTH, 2, D), 0.02),
        'ada_w': nrm(ks[8], (DEPTH, D, 6 * D), 0.5 * D ** -0.5),
        'ada_b': nrm(ks[9], (DEPTH, 6 * D), 0.02),
        'hgrn_w_in': nrm(ks[10], (N_HGRN_LAYERS, D, 2 * HGRN_FD + 2 * HGRN_ID), D ** -0.5),
        'hgrn_lb': 1.0 + nrm(ks[11], (N_HGRN_LAYERS, HGRN_FD), 0.1),
        'hgrn_gnorm': 1.0 + nrm(ks[12], (N_HGRN_LAYERS, HGRN_DV), 0.02),
        'hgrn_w_out': nrm(ks[13], (N_HGRN_LAYERS, HGRN_ID, D), HGRN_ID ** -0.5),
        'ssm_a_re': -0.5 + nrm(ks[14], (N_SSM_LAYERS, g, p), 0.01),
        'ssm_a_im': math.pi * jnp.arange(p, dtype=jnp.float32) + nrm(ks[15], (N_SSM_LAYERS, g, p), 0.01),
        'ssm_log_dt': jax.random.uniform(ks[16], (N_SSM_LAYERS, g), jnp.float32, math.log(1e-3), math.log(1e-1)),
        'ssm_b_re': nrm(ks[17], (N_SSM_LAYERS, g, p, sg), (2 * sg) ** -0.5),
        'ssm_b_im': nrm(ks[18], (N_SSM_LAYERS, g, p, sg), (2 * sg) ** -0.5),
        'ssm_c_re': nrm(ks[19], (N_SSM_LAYERS, g, sg, p), (2 * p) ** -0.5),
        'ssm_c_im': nrm(ks[20], (N_SSM_LAYERS, g, sg, p), (2 * p) ** -0.5),
        'ssm_d': nrm(ks[21], (N_SSM_LAYERS, D), 1.0),
        'ssm_w_glu': nrm(ks[22], (N_SSM_LAYERS, D, 2 * D), D ** -0.5),
        'ffn_w_in': nrm(ks[23], (n_dense, D, 2 * D_FF), D ** -0.5),
        'ffn_w_out': nrm(ks[24], (n_dense, D_FF, D), D_FF ** -0.5),
        'moe_w_router': nrm(ks[25], (n_moe, D, N_EXPERTS), D ** -0.5),
        'moe_b_router': nrm(ks[26], (n_moe, N_EXPERTS), 0.01),
        'moe_w_in': nrm(ks[27], (n_moe, N_EXPERTS, D, 2 * D_FF_EXPERT), D ** -0.5),
        'moe_w_out': nrm(ks[28], (n_moe, N_EXPERTS, D_FF_EXPERT, D), D_FF_EXPERT ** -0.5),
        'final_norm_w': 1.0 + nrm(ks[29], (D,), 0.02),
    }

def reference(x_prompt, x_sample, state_hgrn, state_ssm_re, state_ssm_im, c_prompt, c_sample,
              norm_w, ada_w, ada_b, hgrn_w_in, hgrn_lb, hgrn_gnorm, hgrn_w_out,
              ssm_a_re, ssm_a_im, ssm_log_dt, ssm_b_re, ssm_b_im, ssm_c_re, ssm_c_im, ssm_d, ssm_w_glu,
              ffn_w_in, ffn_w_out, moe_w_router, moe_b_router, moe_w_in, moe_w_out, final_norm_w):
    weights = (norm_w, ada_w, ada_b, hgrn_w_in, hgrn_lb, hgrn_gnorm, hgrn_w_out,
               ssm_a_re, ssm_a_im, ssm_log_dt, ssm_b_re, ssm_b_im, ssm_c_re, ssm_c_im, ssm_d, ssm_w_glu,
               ffn_w_in, ffn_w_out, moe_w_router, moe_b_router, moe_w_in, moe_w_out, final_norm_w)
    bsz = x_prompt.shape[0]
    zero_hgrn = jnp.zeros((N_HGRN_LAYERS, bsz, HGRN_HEADS, HGRN_DK, HGRN_DV), jnp.float32)
    zero_ssm = jnp.zeros((N_SSM_LAYERS, bsz, SSM_GROUPS, SSM_STATE), jnp.float32)
    y_prompt, hgrn_p, re_p, im_p = _trunk(x_prompt, c_prompt, zero_hgrn, zero_ssm, zero_ssm, *weights)
    y_sample, hgrn_s, re_s, im_s = _trunk(x_sample, c_sample, state_hgrn, state_ssm_re, state_ssm_im, *weights)
    return (y_prompt, y_sample, hgrn_p, re_p, im_p, hgrn_s, re_s, im_s)


_drawn_inputs = setup_inputs


def setup_inputs(seed=0):
    import zlib

    import numpy as np

    out = dict(_drawn_inputs(seed))
    spreads = {}
    factors = {'state_hgrn': 4.031,
     'norm_w': 2.872,
     'hgrn_gnorm': 4.231,
     'ssm_a_re': 49.06,
     'moe_b_router': 4.182,
     'final_norm_w': 23.719,
     'ssm_c_im': 3.61,
     'ssm_c_re': 4.368}
    for name, (base, spread) in spreads.items():
        noise = np.random.default_rng([zlib.crc32(name.encode()), seed]).standard_normal(out[name].shape)
        drawn = base * np.exp(spread * noise) if base else spread * noise
        out[name] = __import__('jax').numpy.asarray(drawn.astype(out[name].dtype))
    for name, factor in factors.items():
        out[name] = (out[name] * factor).astype(out[name].dtype)
    return out
```

```python
from contextlib import ExitStack

import concourse.bass as bass
from concourse import mybir

F32 = mybir.dt.float32
I32 = mybir.dt.int32
BF16 = mybir.dt.bfloat16
ALU = mybir.AluOpType
ACT = mybir.ActivationFunctionType
AX = mybir.AxisListType

P = 128
D = 1024
KT = D // P
NP = 256
NB = 8
NS = 8
T = NP + NB * NS
TT = 3
TOK = [P, P, NB * NS]
NC = 1 + NB
H = 8
BLK = 8
NBLK = P // BLK
FF = 2816
FT = FF // P
NE = 8
GP = 32
EPS = 1e-6
SLAB = 2048
RING = 4
XRING = 12
CAP = 112
PASSES = -(-T // CAP)
TWO_PI = 6.283185307179586
PI_A, PI_B, PI_C = 6.28125, 0.0019350051879882812, 3.0199157e-07
ROUND = 12582912.0

C_ID, C_BEFORE, C_ONE, C_CAUSAL = (128 * i for i in range(4))
C_SAMPLE = 512
C_KEEP = 520
C_PAR = 840
C_IOTA = 842
C_W = 970


class Steps:

    def __init__(self, eng, done, base=0):
        self.eng, self.done, self.base, self.n = eng, done, base, 0

    def __call__(self, ins):
        self.n += 1
        ins.then_inc(self.done, 1)
        self.eng.wait_ge(self.done, self.base + self.n)


def trunk(nc, I, outs, prep):
    with ExitStack() as ctx:
        def sb(name, shape, dt=F32):
            return ctx.enter_context(nc.sbuf_tensor(name, shape, dt))

        sems = {}

        def sem(name):
            if name not in sems:
                sems[name] = ctx.enter_context(nc.semaphore(name))
            return sems[name]

        PS = ctx.enter_context(nc.psum_tensor("PS", [P, 8, 512], F32))

        const = sb("const", [P, C_W])
        xT = sb("xT", [P, KT, T])
        hT = sb("hT", [P, KT, T])
        mod = sb("mod", [P, 96, NC])
        siluc = sb("siluc", [P, KT, NC])
        vecs = sb("vecs", [P, 49])
        adab = sb("adab", [P, 96])
        scale_a = sb("scale_a", [P, KT, NC])
        rstd = sb("rstd", [P, T])
        root = sb("root", [P, T])
        gtmp = sb("gtmp", [P, KT * NB * NS])
        work = sb("work", [P, 1024])
        acts = work[:, 0:2 * T].rearrange("p (s t) -> p s t", s=2)
        gated = work[:, 2 * T:3 * T]
        modrow = work[0:NC, :].rearrange("p (s n) -> p s n", s=2)
        sT = sb("sT", [P, 19, GP])
        ring = sb("ring", [P, RING, SLAB])
        zero16 = sb("zero16", [P, 512], BF16)
        wr = sb("wr", [P, KT, NE])
        br = sb("br", [1, NE])
        epst = sb("epst", [P, 1])
        npass = sb("npass", [1, 1], I32)
        AR = 34380
        arena = sb("arena", [P, AR])

        def ar(off, *shape, parts=P):
            n = 1
            for k in shape:
                n *= k
            assert off + n <= AR, (off + n, AR)
            v = arena[0:parts, off:off + n]
            if len(shape) == 1:
                return v
            names = "abcd"[:len(shape)]
            return v.rearrange(f"p ({' '.join(names)}) -> p {' '.join(names)}", **dict(zip(names, shape)))

        ident = const[:, C_ID:C_ID + P]

        rot_c = ar(7168, GP, NP)
        rot_s = ar(7168 + GP * NP, GP, NP)
        keep5 = 7168 + 2 * GP * NP
        bbt = [ar(keep5 + 1024 * i, KT, P) for i in range(2)]
        cct = [ar(keep5 + 2048 + 1024 * i, KT, P) for i in range(2)]
        x0T = [ar(keep5 + 4096 + 256 * i, NB, GP) for i in range(2)]
        addT = [ar(keep5 + 4608 + 256 * i, NB, GP) for i in range(2)]
        KEPT = 5120
        kept = ar(keep5, KEPT)
        magk = ar(keep5 + KEPT, GP, NB * NS)
        s5w = keep5 + KEPT + GP * NB * NS
        bnat = [ar(0 + 512 * i, GP, 16) for i in range(2)]
        cnat = [ar(1024 + 512 * i, KT, 64) for i in range(2)]
        bexp = [ar(2048 + 1024 * i, KT, P) for i in range(2)]
        cexp = [ar(4096 + 1024 * i, KT, P) for i in range(2)]
        x0n = [ar(6144 + 256 * i, 2, P) for i in range(2)]
        xin = ar(8192, TT, D)
        crow = ar(12288, D, parts=NC)
        rowA = ar(13312, P, parts=49)
        rowB = ar(13440, P, parts=96)
        ssr = ar(13600, 46, P, parts=GP)
        t512 = [ar(19500 + 512 * i, GP, 16) for i in range(2)]
        lamT = [ar(20600 + 32 * i, GP) for i in range(2)]
        ub = [[ar(1280 * s + 640 * a, 2, T) for a in range(2)] for s in range(2)]
        vb = [[ar(2560 + 1280 * s + 640 * a, 2, T) for a in range(2)] for s in range(2)]
        zb = [ar(5120 + 640 * a, 2, T) for a in range(2)]
        fin = [ar(6400 + 288 * i, 9, GP) for i in range(2)]
        wp = [ar(s5w + 640 * a, 2, T) for a in range(2)]
        wd = [ar(s5w + 1280 + 640 * a, 2, T) for a in range(2)]
        fout = ar(s5w + 2560, 6, P)
        rtmp = [ar(s5w, GP, 32), ar(s5w + 1024, GP, 32)]
        W8 = KT * T
        hq, hg, hk, hf, hb = (ar(W8 * i, H, T) for i in range(5))
        hbflat = ar(W8 * 4, W8)
        o0 = 5 * W8
        hv = ar(o0, TT, D)
        hkt = ar(o0 + 3072, TT, D)
        ea = [ar(o0 + 6144 + 1024 * i, H, P) for i in range(3)]
        qblk = ar(o0 + 9216, H, P)
        scores = ar(o0 + 10240, H, P)
        st1 = ar(o0 + 11264, H, P)
        vmask = ar(o0 + 12288, NB, P)
        st0 = ar(o0 + 13312, NB, H, P)
        decp = ar(o0 + 21504, H)
        decs = ar(o0 + 21512, H, NB)
        mid = ar(0, FT, T)
        midf = ar(0, FT * T)
        NX = XRING - RING
        xring = ar(0, NX, SLAB)
        m0 = NX * SLAB
        htok = ar(m0, TT, D)
        hexp = ar(m0 + 3072, KT, CAP)
        m1 = m0 + 3072 + KT * CAP
        emid = ar(m1, FT, CAP)
        m2 = m1 + FT * CAP
        sig = ar(m2, 2, 2 * CAP)
        pick = ar(m2 + 4 * CAP, TT, CAP)
        pickg = ar(m2 + 7 * CAP, TT, CAP)
        pickT = ar(m2 + 10 * CAP, T)
        yexp = ar(m2 + 10 * CAP + T, D)
        macc = ar(m2 + 10 * CAP + T + D, KT, T)
        rt = ar(m2 + 10 * CAP + T + D + W8, 12, TT, NE)
        rm = ar(m2 + 10 * CAP + T + D + W8 + 12 * TT * NE, 8, TT)
        yout = htok

        def bc(ap, axis, n):
            return ap.unsqueeze(axis).to_broadcast(list(ap.shape[:axis]) + [n] + list(ap.shape[axis:]))

        def layer_mod(layer, part):
            a = layer * 48 + part * 8
            return mod[:, a:a + 8, :]

        n_mod = (8, 24, 16)
        s_mod0 = 0
        s_hin = s_mod0 + n_mod[0]
        s_mod1 = s_hin + 16
        s_hout = s_mod1 + n_mod[1]
        s_fin = s_hout + 4
        s_fout = s_fin + 22
        s_mod2 = s_fout + 16
        s_glu = s_mod2 + n_mod[2]
        slab_in = [sem(f"slab_in{i}") for i in range(RING)]
        slab_credit = sem("slab_credit")

        order = [("g", 0), ("u", 0)]
        NST = FT // 2
        for s in range(1, NST):
            order += [("g", s), ("u", s), ("o", s - 1)]
        order += [("o", NST - 1)]
        NSL = len(order)
        eindex = {k: j for j, k in enumerate(order)}
        uses = [sum(1 for j in range(NSL) if j % XRING == s) for s in range(XRING)]

        def eslab(slot):
            return ring[:, slot, :] if slot < RING else xring[:, slot - RING, :]

        units = [(2, "r", m) for m in range(BLK)]
        for i in range(2):
            for m in range(BLK):
                units += [(i, "J", J) for J in (2 * m + 1, 2 * m + 2) if J < NBLK] + [(i, "r", m)]
        tiles = (2, 0, 1)
        unit_end = {i: max(u for u, x in enumerate(units) if x[0] == i) + 1 for i in range(TT)}
        unit_first = {i: min(u for u, x in enumerate(units) if x[0] == i) for i in range(TT)}
        o_part = {2: 0, 0: 1, 1: 3}
        sample_at = {BLK + 2 * h: h for h in range(H)}
        mod_lag_rows, mod_lag_turn, mod_lag_bias = 2, 3, 4
        pairs0, pairs1, pairs2 = range(0, 4), range(4, 16), range(16, 24)

        def finals(eng, A, w):
            eng.wait_ge(sem("xs_ready"), w + 1)
            for a in range(2):
                v = vb[w % 2][a]
                A(fin[a][:, 0, 2 * w:2 * w + 2], v[:, :, NP - 1], ACT.Copy)
                last = A(fin[a][:, 1:9, 2 * w:2 * w + 2].rearrange("p b j -> p j b"), v[:, :, NP + NS - 1::NS], ACT.Copy)
            last.then_inc(sem("fin_states"), 1)

        def rotate(step, tt, dst, src, tmp, w, op_re, op_im, which=(0, 1)):
            gs = slice(2 * w, 2 * w + 2)

            def parts(x):
                s = x[:, :, NP:T].rearrange("p j (b t) -> p j b t", b=NB)
                return [x[:, :, 0:NP], s]

            tabs = [[tb[:, gs, :], bc(tb[:, gs, 0:NS], 2, NB)] for tb in (rot_c, rot_s)]
            for q in which:
                both = [parts(x)[q] for x in (*src, *tmp, *dst)]
                re, im, t0, t1, dr, di = both
                c, s = tabs[0][q], tabs[1][q]
                step(tt(t0, re, c, ALU.mult))
                step(tt(t1, im, s, ALU.mult))
                step(tt(dr, t0, t1, op_re))
                step(tt(t0, im, c, ALU.mult))
                step(tt(t1, re, s, ALU.mult))
                step(tt(di, t0, t1, op_im))

        block = ctx.enter_context(nc.Block())

        @block.sync
        def _(sp):
            def put(n, src, dst=None, more=0):
                sp.wait_ge(slab_credit, n + 1 + more)
                if dst is None:
                    dst = ring[:, n % RING, :].rearrange("p (k c) -> p k c", k=KT)
                sp.dma_start(dst, src).then_inc(slab_in[n % RING], 16)

            def load(dst, src, name):
                sp.dma_start(dst, src).then_inc(sem(name), 16)

            load(const[:], I["constants"], "ld_const")
            load(crow[0:1, :], I["c_prompt"], "ld_c")
            load(crow[1:NC, :], I["c_sample"], "ld_c")
            load(rowA[0:32, :], I["norm_w"].rearrange("l s (k p) -> (l s k) p", p=P), "ld_rows")
            load(rowA[32:40, :], I["final_norm_w"].rearrange("(k p) -> k p", p=P), "ld_rows")
            load(rowA[40:48, :], I["ssm_d"].rearrange("l (k p) -> (l k) p", p=P), "ld_rows")
            load(rowA[48:49, :], I["hgrn_gnorm"], "ld_rows")
            load(rowB, I["ada_b"].rearrange("l (k p) -> (l k) p", p=P), "ld_rows")
            load(xin[:, 0:2, :], I["x_prompt"].rearrange("a (i p) d -> p (a i) d", p=P), "ld_x")
            load(xin[0:64, 2, :], I["x_sample"].rearrange("b t d -> (b t) d"), "ld_x")
            for a, nm in enumerate(("ssm_a_re", "ssm_a_im")):
                load(ssr[:, a, :], I[nm].rearrange("l (g u) s -> (l g) (u s)", u=2), "ld_ssm")
            load(ssr[:, 2, 0:2], I["ssm_log_dt"].rearrange("l (g u) -> (l g) u", u=2), "ld_ssm")
            ada = I["ada_w"].rearrange("l (k p) n -> p (l k) n", p=P)
            for j in range(n_mod[0]):
                put(j, ada[:, 0:KT, j * 256:j * 256 + 256])
            for a, nm in enumerate(("ssm_b_re", "ssm_b_im")):
                load(bnat[a], I[nm].rearrange("l (g u) s c -> (u s) (l g) c", u=2), "ld_bc")
            for a, nm in enumerate(("ssm_c_re", "ssm_c_im")):
                load(cnat[a], I[nm].rearrange("l (k g) c s -> (g c) (l k) s", g=8), "ld_bc")
            for a, nm in enumerate(("state_ssm_re", "state_ssm_im")):
                load(x0n[a], I[nm].rearrange("l (i b) (g u) s -> (b g) (l i) (u s)", u=2, i=2), "ld_bc")
            load(wr[:], I["moe_w_router"].rearrange("l (k p) e -> p (l k) e", p=P), "ld_router")
            load(br[:], I["moe_b_router"], "ld_router")
            hw = I["hgrn_w_in"].rearrange("l (k p) n -> p (l k) n", p=P)
            n = s_hin
            for sec in (0, 3, 1, 2):
                for j in range(4):
                    put(n, hw[:, :, sec * D + j * 256:sec * D + j * 256 + 256])
                    n += 1
            with sp.Fori(0, 4) as i:
                for j in range(4):
                    put(s_mod1 + j, ada[:, 0:KT, bass.ds(i * 1024 + 2048 + j * 256, 256)], more=i * 4)
            with sp.Fori(0, 2) as i:
                for j in range(4):
                    put(s_mod1 + 16 + j, ada[:, KT:2 * KT, bass.ds(i * 1024 + j * 256, 256)], more=i * 4)
            how = I["hgrn_w_out"].rearrange("l (k p) n -> p (l k) n", p=P)
            for j in range(4):
                put(s_hout + j, how[:, :, j * 256:j * 256 + 256])
            fw = I["ffn_w_in"].rearrange("l (k p) n -> p (l k) n", p=P)
            for m in range(2):
                put(s_fin + m, fw[:, :, m * FF:m * FF + 256])
            sp.wait_ge(sem("state1_ready"), 2)
            sp.dma_start(outs[2].rearrange("l b h d e -> d (l b h) e"), st1).then_inc(sem("hgrn_out"), 16)
            sp.wait_ge(sem("state0_new"), H)
            sp.dma_start(outs[5].rearrange("l b h d e -> d (l b h) e"),
                         st0.rearrange("p b h e -> p (b h) e")).then_inc(sem("hgrn_out"), 16)
            sp.wait_ge(sem("hgrn_out"), 32)
            sp.wait_ge(sem("o_ready"), 1)
            load(kept, prep, "ld_kept")
            with sp.Fori(0, 5) as i:
                for j in range(4):
                    col = (j % 2) * FF + (1 + j // 2) * 256
                    put(s_fin + 2 + j, fw[:, :, bass.ds(i * 512 + col, 256)], more=i * 4)
            fo = I["ffn_w_out"].rearrange("l (k p) n -> p (l k) n", p=P)
            with sp.Fori(0, 4) as i:
                for j in range(4):
                    half = j % 2
                    n = s_fout + j
                    put(n, fo[:, half * 11:half * 11 + 11, bass.ds(i * 256 + (j // 2) * P, P)],
                        ring[:, n % RING, 0:11 * P].rearrange("p (k c) -> p k c", k=11), more=i * 4)
            with sp.Fori(0, 4) as i:
                for j in range(4):
                    put(s_mod2 + j, ada[:, KT:2 * KT, bass.ds(i * 1024 + 2048 + j * 256, 256)], more=i * 4)
            gw = I["ssm_w_glu"].rearrange("l (k p) n -> p (l k) n", p=P)
            with sp.Fori(0, 2) as i:
                for j in range(4):
                    put(s_glu + j, gw[:, :, bass.ds(i * 512 + (j % 2) * D + (j // 2) * 256, 256)], more=i * 4)
            sp.wait_ge(sem("fout_ready"), 1)
            for a in range(2):
                sp.dma_start(outs[3 + a].rearrange("l b (g u) s -> (l b g) (u s)", u=2), fout[0:GP, a, :]).then_inc(sem("s5_out"), 16)
                sp.dma_start(outs[6 + a].rearrange("l (i b) (g u) s -> (b g) (l i) (u s)", i=2, u=2),
                             fout[:, 2 + 2 * a:4 + 2 * a, :]).then_inc(sem("s5_out"), 16)
            sp.wait_ge(sem("passes_known"), 1)
            n_pass = sp.value_load(npass[0:1, 0:1], min_val=1, max_val=PASSES)
            wi = I["moe_w_in"].rearrange("l e (k p) n -> p (l e k) n", p=P)
            wo = I["moe_w_out"].rearrange("l e (k p) n -> p (l e k) n", p=P)
            with sp.Fori(0, n_pass) as ps:
                with sp.Fori(0, NE) as e:
                    it = ps * NE + e
                    for j, (kind, s) in enumerate(order):
                        former = j - XRING + 1 + NSL if j >= XRING else \
                            max(x for x in range(NSL) if x % XRING == j) + 1
                        sp.wait_ge(sem("expert_credit"), it * NSL + former)
                        dst = eslab(j % XRING)
                        if kind == "o":
                            src = wo[:, bass.ds(e * FT + s * 2, 2), :]
                            dst = dst.rearrange("p (k c) -> p k c", k=2)
                        else:
                            col = (FF if kind == "u" else 0) + s * 256
                            src = wi[:, bass.ds(e * KT, KT), col:col + 256]
                            dst = dst.rearrange("p (k c) -> p k c", k=KT)
                        sp.dma_start(dst, src).then_inc(sem(f"expert_in{j % XRING}"), 16)
            sp.wait_ge(sem("y_ready"), 6)
            sp.dma_start(outs[0].rearrange("a (i p) d -> p (a i) d", p=P), yout[:, 0:2, :]).then_inc(sem("stored"), 16)
            sp.dma_start(outs[1].rearrange("b t d -> (b t) d"), yout[0:64, 2, :]).then_inc(sem("stored"), 16)
            sp.wait_ge(sem("stored"), 32)
            sp.wait_ge(sem("s5_out"), 64)

        @block.tensor
        def _(pe):
            def tr(out, in_, k):
                return pe.matmul(out, in_, ident[0:k, 0:k], start=True, stop=True)

            def arrived(n, more=0):
                pe.wait_ge(slab_in[n % RING], (n // RING + 1) * 16 + more * 16)

            pe.sem_inc(slab_credit, RING - 1)
            pe.wait_ge(sem("ld_const"), 16)
            pe.wait_ge(sem("ld_rows"), 80)
            tr(PS[:, 4, 0:49], rowA, 49)
            tr(PS[:, 4, 64:160], rowB, 96).then_inc(sem("vecs_psum"), 1)
            pe.wait_ge(sem("silu_c"), 1)
            for k in range(KT):
                last = tr(PS[:, 5, 16 * k:16 * k + NC], crow[:, k * P:(k + 1) * P], NC)
            last.then_inc(sem("siluc_psum"), 1)
            pe.wait_ge(sem("ld_x"), 32)
            for i in range(TT):
                for half in range(2):
                    if i == 2:
                        pe.wait_ge(sem("x_turned"), half + 1)
                    for k in range(4):
                        kk = half * 4 + k
                        last = tr(PS[:, 2 * (i % 2) + half, k * P:k * P + TOK[i]],
                                  xin[0:TOK[i], i, kk * P:(kk + 1) * P], TOK[i])
                    last.then_inc(sem("x_psum"), 1)
            pe.wait_ge(sem("x_turned"), 6)
            pe.wait_ge(sem("siluc_ready"), 1)

            def mod_rows(q, half, bank):
                n = q * 2 + half
                n += s_mod0 if q in pairs0 else s_mod1 - 8 if q in pairs1 else s_mod2 - 32
                if half == 0 and q:
                    pe.wait_ge(sem("mod_rows_read"), q)
                arrived(n)
                for k in range(KT):
                    last = pe.matmul(PS[0:NC, bank, half * 256:half * 256 + 256], siluc[:, k, :],
                                     ring[:, n % RING, k * 256:k * 256 + 256], start=(k == 0), stop=(k == KT - 1))
                    if k == 0:
                        last.then_inc(slab_credit, 1)
                if half:
                    last.then_inc(sem("mod_rows_psum"), 1)

            def mod_turn(q, bank):
                pe.wait_ge(sem("mod_rows_read"), q + 1)
                if q:
                    pe.wait_ge(sem("mod_ready"), q)
                for c in range(4):
                    last = tr(PS[:, bank, c * NC:(c + 1) * NC], modrow[:, q % 2, c * P:(c + 1) * P], NC)
                last.then_inc(sem("mod_turn_psum"), 1)

            for q in pairs0:
                mod_rows(q, 0, q % 2)
                mod_rows(q, 1, q % 2)
                if q:
                    mod_turn(q - 1, 6)
            mod_turn(pairs0[-1], 6)
            pe.wait_ge(sem("mod_ready"), len(pairs0))
            pe.wait_ge(sem("ssm_rows"), 1)
            for m in range(19):
                last = tr(PS[:, 4 + m // 10, (m % 10) * GP:(m % 10) * GP + GP], ssr[:, 16 + m, :], GP)
            last.then_inc(sem("ssm_psum"), 1)
            pe.wait_ge(sem("ld_bc"), 96)
            for a in range(2):
                for m in range(2):
                    last = tr(PS[:, 6, (a * 2 + m) * P:(a * 2 + m + 1) * P], x0n[a][:, m, :], P)
            last.then_inc(sem("x0_psum"), 1)
            pe.wait_ge(sem("mats_made"), 1)
            g = 0
            for src in (bexp[0], bexp[1], cexp[0], cexp[1]):
                for half in range(2):
                    if g >= 4:
                        pe.wait_ge(sem("mats_turned"), g - 3)
                    for k in range(4):
                        last = tr(PS[:, (2, 3, 4, 7)[g % 4], k * P:(k + 1) * P], src[:, half * 4 + k, :], P)
                    last.then_inc(sem("mats_psum"), 1)
                    g += 1
            pe.wait_ge(sem("mats_turned"), 8)
            norms = [0]

            def norm():
                norms[0] += 1
                pe.wait_ge(sem("squares"), norms[0])
                for k in range(KT):
                    last = pe.matmul(PS[:, 7, 0:T], const[:, C_ONE:C_ONE + P], hT[:, k, :],
                                     start=(k == 0), stop=(k == KT - 1))
                last.then_inc(sem("sum_psum"), 1)
                pe.wait_ge(sem("h_ready"), norms[0])

            norm()
            with pe.Fori(0, 3) as s:
                for h in range(H):
                    pe.wait_ge(sem("hin_credit"), s * H + h + 1)
                    if h % 2 == 0:
                        pe.wait_ge(slab_in[h // 2], s * 16 + (s_hin // RING + 1) * 16)
                    for k in range(KT):
                        last = pe.matmul(PS[:, h % 4, 0:T],
                                         ring[:, h // 2, k * 256 + (h % 2) * P:k * 256 + (h % 2) * P + P],
                                         hT[:, k, :], start=(k == 0), stop=(k == KT - 1))
                        if h % 2 == 0 and k == 0:
                            last.then_inc(slab_credit, 1)
                    last.then_inc(sem("hin_psum"), 1)
            g = 3 * H
            for j in range(4):
                arrived(s_hin + 12 + j)
                for i in range(TT):
                    pe.wait_ge(sem("hin_credit"), g + 1)
                    for k in range(KT):
                        last = pe.matmul(PS[0:TOK[i], g % 4, 0:256], hT[:, k, i * P:i * P + TOK[i]],
                                         ring[:, j, k * 256:k * 256 + 256], start=(k == 0), stop=(k == KT - 1))
                        if i == 0 and k == 0:
                            last.then_inc(slab_credit, 1)
                    last.then_inc(sem("hin_psum"), 1)
                    g += 1
            pe.wait_ge(sem("kend_ready"), 1)
            g = 0
            for i in range(TT):
                for half in range(2):
                    if g >= 2:
                        pe.wait_ge(sem("kt_ready"), g - 1)
                    for k in range(4):
                        h = half * 4 + k
                        last = tr(PS[0:TOK[i], 6 + g % 2, k * P:(k + 1) * P], hT[:, h, i * P:i * P + TOK[i]], P)
                    last.then_inc(sem("kt_psum"), 1)
                    g += 1
            pe.wait_ge(sem("kt_ready"), 6)
            for u, (i, kind, m) in enumerate(units):
                n = TOK[i]
                nb = n // BLK
                ti = tiles.index(i)
                if kind == "J" and m == 1:
                    pe.wait_ge(sem("scores_ready"), ti)
                    for half in range(2):
                        pe.matmul(PS[:, half, :], zero16[:, 0:P], zero16[:], start=True, stop=False, skip_group_check=True)
                    pe.wait_ge(sem("qblk_ready"), i + 1)
                pe.wait_ge(sem("keys_ready"), u + 1)
                for h in range(H):
                    if kind == "J":
                        c = (h % 4) * P + BLK * m
                        last = pe.matmul(PS[0:BLK * m, h // 4, c:c + BLK], ea[u % 3][:, h, 0:BLK * m],
                                         qblk[:, h, BLK * m:BLK * m + BLK], start=False,
                                         stop=(m == NBLK - 1 and h % 4 == 3), skip_group_check=True)
                    else:
                        at = (m * H + h) * nb
                        last = pe.matmul(PS[0:n, 2 + at // 512, at % 512:at % 512 + nb], ea[u % 3][:, h, 0:n],
                                         hq[:, h, i * P + m:i * P + n:BLK], start=True, stop=True,
                                         skip_group_check=True)
                last.then_inc(sem("keys_used"), 1)
                if u < n_mod[1]:
                    mod_rows(pairs1[u // 2], u % 2, 5)
                if u >= mod_lag_turn + 1 and (u - mod_lag_turn) % 2 and (u - mod_lag_turn) // 2 < len(pairs1):
                    mod_turn(pairs1[(u - mod_lag_turn) // 2], 4)
                if u in sample_at:
                    h = sample_at[u]
                    pe.wait_ge(sem("vmask_ready"), h + 1)
                    if h:
                        pe.wait_ge(sem("state0_new"), h)
                    for half in range(2):
                        last = pe.matmul(PS[:, 6 + half, :], hkt[0:64, 2, h * P:(h + 1) * P],
                                         vmask[0:64, half * 4:half * 4 + 4, :], start=True, stop=True)
                    last.then_inc(sem("state0_psum"), 1)
                if u + 1 != unit_end[i]:
                    continue
                pe.wait_ge(sem("scores_ready"), ti + 1)
                if i == 1:
                    pe.wait_ge(sem("state1_ready"), 1)
                if i == 2:
                    pe.wait_ge(sem("ld_state"), 16)
                    pe.wait_ge(sem("qfull_ready"), 1)
                pe.wait_ge(sem("mod_ready"), len(pairs0) + min(len(pairs1), (u - mod_lag_bias + 1) // 2))
                for part in range(H * n // 512):
                    op = o_part[i] + part
                    if op:
                        pe.wait_ge(sem("o_read"), op)
                    for h in range(part * 512 // n, (part + 1) * 512 // n):
                        at = (h * n) % 512
                        o = PS[:, 4, at:at + n]
                        last = pe.matmul(o, hv[0:n, i, h * P:(h + 1) * P], scores[0:n, h, 0:n], start=True,
                                         stop=(i == 0), skip_group_check=True)
                        if i == 1:
                            last = pe.matmul(o, st1[:, h, :], hf[:, h, P:2 * P], start=False, stop=True,
                                             skip_group_check=True)
                        if i == 2:
                            for b in range(NB):
                                last = pe.matmul(o[:, b * NS:(b + 1) * NS], st0[:, b, h, :],
                                                 hf[:, h, NP + b * NS:NP + (b + 1) * NS],
                                                 start=False, stop=(b == NB - 1), skip_group_check=True)
                    last.then_inc(sem("o_psum"), 1)
                if i < 2:
                    if i == 0:
                        pe.wait_ge(sem("state0_new"), H)
                    for h in range(H):
                        last = pe.matmul(PS[:, 6 + h // 4, (h % 4) * P:(h % 4 + 1) * P], hkt[:, i, h * P:(h + 1) * P],
                                         hv[:, i, h * P:(h + 1) * P], start=True, stop=True)
                    last.then_inc(sem("state_psum"), 1)
            pe.wait_ge(sem("o_squares"), 1)
            for c in range(5):
                last = pe.matmul(PS[:, c, :], const[:, C_ONE:C_ONE + P], hbflat[:, c * 512:(c + 1) * 512],
                                 start=True, stop=True)
            last.then_inc(sem("o_sums"), 1)
            pe.wait_ge(sem("o_ready"), 1)
            for dt in range(KT):
                n = s_hout + dt // 2
                if dt >= 4:
                    pe.wait_ge(sem("hout_read"), dt - 3)
                if dt % 2 == 0:
                    arrived(n)
                for k in range(KT):
                    last = pe.matmul(PS[:, dt % 4, 0:T], ring[:, n % RING, k * 256 + (dt % 2) * P:k * 256 + (dt % 2) * P + P],
                                     hT[:, k, :], start=(k == 0), stop=(k == KT - 1))
                    if dt % 2 == 0 and k == 0:
                        last.then_inc(slab_credit, 1)
                last.then_inc(sem("hout_psum"), 1)
            norm()

            def gate_up(n, tile, more_tiles, used):
                for sub in range(2):
                    t = tile + sub
                    pe.wait_ge(sem("fin_credit"), t + 1 + more_tiles)
                    for m in range(2):
                        for k in range(KT):
                            last = pe.matmul(PS[:, 2 * (t % 2) + m, 0:T],
                                             ring[:, (n + m) % RING, k * 256 + sub * P:k * 256 + sub * P + P],
                                             hT[:, k, :], start=(k == 0), stop=(k == KT - 1))
                            if sub == 0 and m == 0 and k == 0:
                                last.then_inc(slab_credit, used)
                        last.then_inc(sem("gate_psum" if m == 0 else "up_psum"), 1)

            arrived(s_fin)
            arrived(s_fin + 1)
            gate_up(s_fin, 0, 0, 1)
            with pe.Fori(0, 5) as i:
                for pr in range(2):
                    n = s_fin + 2 + 2 * pr
                    arrived(n, i)
                    arrived(n + 1, i)
                    gate_up(n, 2 + 2 * pr, i * 4, 2)
            pe.wait_ge(sem("mid_ready"), FT)
            with pe.Fori(0, 4) as i:
                for c in range(2):
                    n = s_fout + 2 * c
                    pe.wait_ge(sem("fout_credit"), i * 2 + c + 1)
                    arrived(n, i)
                    arrived(n + 1, i)
                    for k in range(FT):
                        last = pe.matmul(PS[:, c, 0:T], ring[:, (n + k // 11) % RING, (k % 11) * P:(k % 11 + 1) * P],
                                         mid[:, k, :], start=(k == 0), stop=(k == FT - 1))
                        if k == 0:
                            last.then_inc(slab_credit, 2)
                    last.then_inc(sem("fout_psum"), 1)
            norm()
            pe.wait_ge(sem("ld_kept"), 16)

            def states_in(w):
                for j in range(2):
                    gp = 2 * w + j
                    k, q = gp // 4, 32 * (gp % 4)
                    for a in range(2):
                        g = gp * 2 + a
                        if g >= 4:
                            pe.wait_ge(sem("bu_read"), g - 3)
                        pe.matmul(PS[:, g % 4, 0:T], bbt[a][q:q + 32, k, :], hT[q:q + 32, k, :],
                                  start=True, stop=True).then_inc(sem("bu_psum"), 1)

            def states_out(w):
                k = w // 2
                pe.wait_ge(sem("xs_ready"), w + 1)
                if w % 2 == 0 and k >= 2:
                    pe.wait_ge(sem("y5_read"), k - 1)
                for j in range(2):
                    q = 32 * ((2 * w + j) % 4)
                    for a in range(2):
                        last = pe.matmul(PS[q:q + 32, 4 + k % 2, 0:T], cct[a][:, k, q:q + 32],
                                         vb[w % 2][a][:, j, :], start=(a == 0), stop=(a == 1), skip_group_check=True)
                last.then_inc(sem("xs_used"), 1)

            NW = GP // 2
            for w in range(NW):
                states_in(w)
                mod_rows(pairs2[w // 2], w % 2, 6)
                if w:
                    states_out(w - 1)
                if w > 1 and w % 2 == 0:
                    mod_turn(pairs2[w // 2 - 1], 7)
            states_out(NW - 1)
            mod_turn(pairs2[-1], 7)
            pe.wait_ge(sem("mod_ready"), 24)
            pe.wait_ge(sem("fin_states"), NW)
            for a in range(2):
                tr(PS[0:GP, 6, a * P:a * P + P], fin[a][:, 0, :], P)
                for m in range(2):
                    last = tr(PS[:, 7, (a * 2 + m) * P:(a * 2 + m + 1) * P],
                              fin[a][:, 1 + 4 * m:5 + 4 * m, :].rearrange("p b g -> p (b g)"), P)
            last.then_inc(sem("fin_psum"), 1)
            pe.wait_ge(sem("z_ready"), 1)
            with pe.Fori(0, 2) as i:
                for pr in range(2):
                    n = s_glu + 2 * pr
                    arrived(n, i)
                    arrived(n + 1, i)
                    for sub in range(2):
                        pe.wait_ge(sem("glu_credit"), i * 4 + pr * 2 + sub + 1)
                        for m in (1, 0):
                            for k in range(KT):
                                last = pe.matmul(PS[:, 2 * sub + m, 0:T],
                                                 ring[:, (n + m) % RING, k * 256 + sub * P:k * 256 + sub * P + P],
                                                 hT[:, k, :], start=(k == 0), stop=(k == KT - 1))
                                if sub == 0 and m == 1 and k == 0:
                                    last.then_inc(slab_credit, 2)
                            last.then_inc(sem("glu_b_psum" if m else "glu_a_psum"), 1)
            norm()
            pe.sem_inc(sem("expert_credit"), NSL - 1)
            pe.wait_ge(sem("ld_router"), 32)
            for i in range(TT):
                n = TOK[i]
                for k in range(KT):
                    pe.matmul(PS[0:n, 4, 16 * i:16 * i + NE], hT[:, k, i * P:i * P + n], wr[:, k, :],
                              start=(k == 0), stop=False)
                last = pe.matmul(PS[0:n, 4, 16 * i:16 * i + NE], const[0:1, C_ONE:C_ONE + n], br[:],
                                 start=False, stop=True)
            last.then_inc(sem("logits"), 1)
            g = 0
            for i in range(TT):
                for half in range(2):
                    if g >= 4:
                        pe.wait_ge(sem("htok_read"), g - 3)
                    for k in range(4):
                        last = tr(PS[0:TOK[i], g % 4, k * P:(k + 1) * P], hT[:, half * 4 + k, i * P:i * P + TOK[i]], P)
                    last.then_inc(sem("htok_psum"), 1)
                    g += 1
            pe.wait_ge(sem("chosen"), 1)
            for i in range(TT):
                n = TOK[i]
                for m in range(i):
                    pe.matmul(PS[0:n, 5, 16 * i:16 * i + NE], const[:, C_ONE:C_ONE + n], rt[:, 2, m, :],
                              start=(m == 0), stop=False)
                pe.matmul(PS[0:n, 5, 16 * i:16 * i + NE], const[0:n, C_BEFORE:C_BEFORE + n], rt[0:n, 2, i, :],
                          start=(i == 0), stop=True)
            for m in range(TT):
                last = pe.matmul(PS[:, 5, 64:64 + NE], const[0:TOK[m], C_ONE:C_ONE + P], rt[0:TOK[m], 2, m, :],
                                 start=(m == 0), stop=(m == TT - 1))
            last.then_inc(sem("places"), 1)
            pe.wait_ge(sem("htok_read"), 6)
            pe.wait_ge(sem("passes_known"), 1)
            n_pass = pe.value_load(npass[0:1, 0:1], min_val=1, max_val=PASSES)
            with pe.Fori(0, n_pass) as ps:
                with pe.Fori(0, NE) as e:
                    it = ps * NE + e

                    def slab(kind, s):
                        j = eindex[(kind, s)]
                        q = j % XRING
                        pe.wait_ge(sem(f"expert_in{q}"), it * (uses[q] * 16) + (j // XRING + 1) * 16)
                        return eslab(q)

                    pe.wait_ge(sem("pick_ready"), it + 1)
                    for half in range(2):
                        pe.wait_ge(sem("scatter_read"), it * KT + KT - 1 + half)
                        for k in range(4):
                            for i in range(TT):
                                kk = half * 4 + k
                                last = pe.matmul(PS[:, 6 + half, k * P:k * P + CAP], htok[0:TOK[i], i, kk * P:(kk + 1) * P],
                                                 pick[0:TOK[i], i, :], start=(i == 0), stop=(i == TT - 1))
                        last.then_inc(sem("gather_psum"), 1)
                    for i in range(TT):
                        last = tr(PS[0:CAP, 3, i * P:i * P + TOK[i]], pickg[0:TOK[i], i, :], TOK[i])
                    last.then_inc(sem("pickT_psum"), 1)
                    pe.wait_ge(sem("hexp_ready"), it * 2 + 2)

                    def up(s):
                        w = [slab("g", s), slab("u", s)]
                        pe.wait_ge(sem("emid_done"), it * NST + (s - 2 + NST if s >= 3 else (10, 11, 9)[s]))
                        for m in range(2):
                            for c in range(2):
                                for k in range(KT):
                                    last = pe.matmul(PS[:, s % 3, (m * 2 + c) * CAP:(m * 2 + c + 1) * CAP],
                                                     w[m][:, k * 256 + c * P:k * 256 + c * P + P], hexp[:, k, :],
                                                     start=(k == 0), stop=(k == KT - 1))
                                    if c == 0 and k == 0:
                                        last.then_inc(sem("expert_credit"), 1)
                        last.then_inc(sem("eup_psum"), 1)

                    def down(s):
                        w = slab("o", s)
                        pe.wait_ge(sem("emid_done"), it * NST + NST + s + 1)
                        for c in range(2):
                            for half in range(2):
                                last = pe.matmul(PS[0:CAP, 4 + half, :], emid[:, 2 * s + c, :],
                                                 w[:, c * D + half * 512:c * D + half * 512 + 512],
                                                 start=(s == 0 and c == 0), stop=(s == NST - 1 and c == 1))
                                if c == 0 and half == 0:
                                    last.then_inc(sem("expert_credit"), 1)
                        return last

                    up(0)
                    for s in range(1, NST):
                        up(s)
                        down(s - 1)
                    down(NST - 1).then_inc(sem("y_psum"), 1)
                    pe.wait_ge(sem("yexp_ready"), it + 1)
                    pe.wait_ge(sem("pickT_ready"), it + 1)
                    for dt in range(KT):
                        if dt >= 2:
                            pe.wait_ge(sem("scatter_read"), it * KT + KT + dt - 1)
                        pe.matmul(PS[:, 6 + dt % 2, 0:T], yexp[0:CAP, dt * P:(dt + 1) * P], pickT[0:CAP, :],
                                  start=True, stop=True).then_inc(sem("scatter_psum"), 1)
            norm()
            g = 0
            for i in range(TT):
                for half in range(2):
                    if g >= 4:
                        pe.wait_ge(sem("y_ready"), g - 3)
                    for k in range(4):
                        last = tr(PS[0:TOK[i], g % 4, k * P:(k + 1) * P], hT[:, half * 4 + k, i * P:i * P + TOK[i]], P)
                    last.then_inc(sem("y_out_psum"), 1)
                    g += 1

        @block.scalar
        def _(act):
            A = nc.scalar.activation
            step = Steps(act, sem("act_step"))
            norms = [0]

            def norm():
                norms[0] += 1
                if norms[0] == 1:
                    act.wait_ge(sem("x_turned"), 6)
                else:
                    act.wait_ge(sem("x_ready"), norms[0] - 1)
                A(hT[:], xT[:], ACT.Square).then_inc(sem("squares"), 1)
                act.wait_ge(sem("sum_psum"), norms[0])
                act.wait_ge(sem("eps_ready"), 1)
                A(root[:], PS[:, 7, 0:T], ACT.Sqrt, bias=epst[:, 0:1], scale=1.0 / D).then_inc(sem("root_ready"), 1)

            act.wait_ge(sem("ld_c"), 32)
            A(crow, crow, ACT.Silu).then_inc(sem("silu_c"), 1)
            act.wait_ge(sem("ld_ssm"), 48)
            A(ssr[:, 2, 2:4], ssr[:, 2, 0:2], ACT.Exp).then_inc(sem("dt_ready"), 1)
            act.wait_ge(sem("angles"), 1)
            A(ssr[:, 32, :], ssr[:, 43, :], ACT.Exp).then_inc(sem("mag_ready"), 1)
            A(ssr[:, 16:32, :], ssr[:, 16:32, :], ACT.Sin).then_inc(sem("sines"), 1)
            def mod_copy(q, bank):
                act.wait_ge(sem("mod_rows_psum"), q + 1)
                if q > 1:
                    act.wait_ge(sem("mod_turn_psum"), q - 1)
                A(modrow[:, q % 2, :], PS[0:NC, bank, :], ACT.Copy).then_inc(sem("mod_rows_read"), 1)

            for q in pairs0:
                mod_copy(q, q % 2)
            norm()
            act.sem_inc(sem("hin_credit"), 4)
            g = 0
            for dst in (hq, hg):
                for h in range(H):
                    act.wait_ge(sem("hin_psum"), g + 1)
                    A(dst[:, h, :], PS[:, g % 4, 0:T], ACT.Silu).then_inc(sem("hin_credit"), 1)
                    g += 1
            act.wait_ge(sem("prep_stored"), 16)
            act.dma_start(st0.rearrange("p b h e -> p (b h) e"),
                          I["state_hgrn"].rearrange("l b h d e -> d (l b h) e")).then_inc(sem("ld_state"), 16)
            for h in range(H):
                act.wait_ge(sem("hin_psum"), g + 1)
                A(hk[:, h, :], PS[:, g % 4, 0:T], ACT.Sigmoid, scale=-1.0)
                A(hb[:, h, :], PS[:, g % 4, 0:T], ACT.Abs)
                A(hf[:, h, :], PS[:, g % 4, 0:T], ACT.Copy).then_inc(sem("hin_credit"), 1)
                g += 1
            for j in range(4):
                for i in range(TT):
                    act.wait_ge(sem("hin_psum"), g + 1)
                    A(hv[0:TOK[i], i, j * 256:j * 256 + 256], PS[0:TOK[i], g % 4, 0:256], ACT.Copy)\
                        .then_inc(sem("hin_credit"), 1)
                    g += 1
            act.wait_ge(sem("hin_credit"), 4 + g)
            step(A(hb, hb, ACT.Exp, scale=-1.0))
            A(hb, hb, ACT.Ln, bias=1.0).then_inc(sem("softplus_ready"), 1)
            act.wait_ge(sem("b_ready"), 1)
            A(hf, hb, ACT.Exp).then_inc(sem("expb_ready"), 1)
            A(decp, hb[:, :, NP - 1], ACT.Exp).then_inc(sem("dec_ready"), 1)
            A(decs, hb[:, :, NP + NS - 1::NS], ACT.Exp).then_inc(sem("dec_ready"), 1)
            a = 0

            def decay(ap):
                nonlocal a
                act.wait_ge(sem("args_ready"), a + 1)
                A(ap, ap, ACT.Exp).then_inc(sem("decays_ready"), 1)
                a += 1

            decay(hT[:])
            for u, (i, kind, m) in enumerate(units):
                n = TOK[i]
                if kind == "J" and m == 1:
                    decay(qblk[:, :, BLK:])
                decay(ea[u % 3][:, :, 0:BLK * m] if kind == "J" else ea[u % 3][:, :, 0:n])
                if u > mod_lag_rows and (u - mod_lag_rows) % 2 and (u - mod_lag_rows) // 2 < len(pairs1):
                    mod_copy(pairs1[(u - mod_lag_rows) // 2], 5)
                if u + 1 != unit_end[i]:
                    continue
                for part in range(H * n // 512):
                    op = o_part[i] + part
                    act.wait_ge(sem("o_psum"), op + 1)
                    hs = slice(part * 512 // n, (part + 1) * 512 // n)
                    A(hT[:, hs, i * P:i * P + n], PS[:, 4, :].rearrange("p (h t) -> p h t", t=n), ACT.Copy)\
                        .then_inc(sem("o_read"), 1)
                if i == 0:
                    act.wait_ge(sem("state_psum"), 1)
                    A(st1.rearrange("p (c h) e -> p c (h e)", c=2), PS[:, 6:8, :], ACT.Copy).then_inc(sem("state1_ready"), 1)
            act.wait_ge(sem("o_read"), 5)
            A(hbflat, hT[:].rearrange("p h t -> p (h t)"), ACT.Square).then_inc(sem("o_squares"), 1)
            act.wait_ge(sem("o_sums"), 1)
            A(hk.rearrange("p h t -> p (h t)").rearrange("p (c n) -> p c n", c=5), PS[:, 0:5, :], ACT.Sqrt,
              bias=epst[:, 0:1], scale=1.0 / P).then_inc(sem("o_root"), 1)
            norm()
            with act.Fori(0, FT // 2) as i:
                for c in range(2):
                    act.wait_ge(sem("gate_psum"), i * 2 + c + 1)
                    A(acts[:, c, :], PS[:, 2 * c, 0:T], ACT.Silu).then_inc(sem("silu_ready"), 1)
            norm()
            NW = GP // 2
            for w in range(NW):
                for j in range(2):
                    for a_ in range(2):
                        g = (2 * w + j) * 2 + a_
                        act.wait_ge(sem("bu_psum"), g + 1)
                        if w >= 2:
                            act.wait_ge(sem("v_ready"), w - 1)
                            act.wait_ge(sem("u_used"), w - 1)
                        A(ub[w % 2][a_][:, j, :], PS[:, g % 4, 0:T], ACT.Copy).then_inc(sem("bu_read"), 1)
                if w % 2 == 0 and w:
                    mod_copy(pairs2[w // 2 - 1], 6)
                if w:
                    finals(act, A, w - 1)
            mod_copy(pairs2[-1], 6)
            finals(act, A, NW - 1)
            act.wait_ge(sem("fin_psum"), 1)
            A(fout[0:GP, 0:2, :], PS[0:GP, 6, 0:2 * P].rearrange("p (a n) -> p a n", a=2), ACT.Copy)
            A(fout[:, 2:6, :], PS[:, 7, :].rearrange("p (a n) -> p a n", a=4), ACT.Copy).then_inc(sem("fout_ready"), 1)
            act.wait_ge(sem("y5_read"), KT)
            A(hT[:], hT[:], ACT.Gelu_apprx_tanh).then_inc(sem("z_ready"), 1)
            with act.Fori(0, 4) as i:
                for c in range(2):
                    act.wait_ge(sem("glu_b_psum"), i * 2 + c + 1)
                    A(acts[:, c, :], PS[:, 2 * c + 1, 0:T], ACT.Sigmoid).then_inc(sem("sigmoid_ready"), 1)
            norm()
            g = 0
            for i in range(TT):
                for half in range(2):
                    act.wait_ge(sem("htok_psum"), g + 1)
                    A(htok[0:TOK[i], i, half * 512:half * 512 + 512], PS[0:TOK[i], g % 4, :], ACT.Copy)\
                        .then_inc(sem("htok_read"), 1)
                    g += 1
            act.wait_ge(sem("second_less_first"), 1)
            A(rm[:, 5, :], rm[:, 4, :], ACT.Exp).then_inc(sem("second_exp"), 1)
            act.wait_ge(sem("passes_known"), 1)
            n_pass = act.value_load(npass[0:1, 0:1], min_val=1, max_val=PASSES)
            with act.Fori(0, n_pass) as ps:
                with act.Fori(0, NE) as e:
                    it = ps * NE + e
                    for half in range(2):
                        act.wait_ge(sem("gather_psum"), it * 2 + half + 1)
                        A(hexp[:, half * 4:half * 4 + 4, :],
                          PS[:, 6 + half, :].rearrange("p (k n) -> p k n", k=4)[:, :, 0:CAP], ACT.Copy)\
                            .then_inc(sem("hexp_ready"), 1)
                    act.wait_ge(sem("pickT_psum"), it + 1)
                    A(pickT[0:CAP, :], PS[0:CAP, 3, 0:T], ACT.Copy).then_inc(sem("pickT_ready"), 1)
                    for s in range(NST):
                        act.wait_ge(sem("eup_psum"), it * NST + s + 1)
                        A(sig[:, s % 2, :], PS[:, s % 3, 0:2 * CAP], ACT.Silu).then_inc(sem("sig_ready"), 1)
                    act.wait_ge(sem("y_psum"), it + 1)
                    A(yexp[0:CAP, :].rearrange("p (c n) -> p c n", c=2), PS[0:CAP, 4:6, :], ACT.Copy)\
                        .then_inc(sem("yexp_ready"), 1)
            norm()

        @block.vector
        def _(dve):
            V = nc.vector
            step = Steps(dve, sem("dve_step"))

            def tt(out, a, b, op):
                return V.tensor_tensor(out, a, b, op)

            norms = [0]

            def norm(scale_of, shift):
                norms[0] += 1
                n = norms[0]
                if n > 1:
                    dve.wait_ge(sem("h_ready"), n - 1)
                if shift is not None:
                    step(V.scalar_tensor_tensor(scale_a[:], scale_of[1], 1.0, bc(scale_of[0], 2, NC), ALU.add, ALU.mult))
                dve.wait_ge(sem("root_ready"), n)
                step(V.reciprocal(rstd[:], root[:]))
                step(tt(hT[:], xT[:], bc(rstd[:], 1, KT), ALU.mult))
                if shift is None:
                    for k in range(KT):
                        last = V.tensor_scalar(hT[:, k, :], hT[:, k, :], scale_of[0][:, k:k + 1], None, ALU.mult)
                    last.then_inc(sem("h_ready"), 1)
                    return
                s = hT[:, :, NP:].rearrange("p k (b t) -> p k b t", b=NB)
                step(tt(s, s, bc(scale_a[:, :, 1:], 3, NS), ALU.mult))
                V.tensor_tensor(s, s, bc(shift[:, :, 1:], 3, NS), ALU.add)
                for k in range(KT):
                    last = V.tensor_scalar(hT[:, k, 0:NP], hT[:, k, 0:NP], scale_a[:, k, 0:1], shift[:, k, 0:1],
                                           ALU.mult, ALU.add)
                last.then_inc(sem("h_ready"), 1)

            def residual(src, dt, gate, done, sem2=None):
                part = gtmp[:, dt * 64:dt * 64 + 64]
                step(tt(part.rearrange("p (b t) -> p b t", b=NB),
                        src[:, NP:T].rearrange("p (b t) -> p b t", b=NB), bc(gate[:, dt, 1:], 2, NS), ALU.mult))
                V.scalar_tensor_tensor(xT[:, dt, 0:NP], src[:, 0:NP], gate[:, dt, 0:1], xT[:, dt, 0:NP],
                                       ALU.mult, ALU.add)
                last = tt(xT[:, dt, NP:T], xT[:, dt, NP:T], part, ALU.add)
                last.then_inc(done, 1)
                return last

            V.memset(epst[:], EPS).then_inc(sem("eps_ready"), 1)
            V.memset(zero16[:], 0.0).then_inc(sem("zeros"), 1)
            dve.wait_ge(sem("ld_ssm"), 48)
            dve.wait_ge(sem("dt_ready"), 1)
            R = ssr
            two = lambda row: R[:, row, :].rearrange("p (u s) -> p u s", u=2)
            dt_ = bc(R[:, 2, 2:4], 2, 64)
            V.tensor_tensor(two(43), two(0), dt_, ALU.mult)
            step(tt(two(3), two(1), dt_, ALU.mult))
            for k in range(1, 8):
                last = V.tensor_scalar(R[:, 3 + k, :], R[:, 3, :], float(2 ** k), None, ALU.mult)
            step(last)
            an, nn, co, si = R[:, 3:11, :], R[:, 35:43, :], R[:, 16:24, :], R[:, 24:32, :]

            def reduced(out, quarter):
                step(V.tensor_scalar(nn, an, 1.0 / TWO_PI, 0.25 * quarter, ALU.mult, ALU.add))
                step(V.tensor_scalar(nn, nn, ROUND, -ROUND, ALU.add, ALU.add))
                step(V.scalar_tensor_tensor(out, nn, -PI_A, an, ALU.mult, ALU.add))
                step(V.scalar_tensor_tensor(out, nn, -PI_B, out, ALU.mult, ALU.add))
                step(V.scalar_tensor_tensor(out, nn, -PI_C, out, ALU.mult, ALU.add))
                if quarter:
                    step(V.tensor_scalar(out, out, TWO_PI / 4, None, ALU.add))
                return V.tensor_scalar(out, out, 3.1415925, -3.1415925, ALU.min, ALU.max)

            step(reduced(si, 0))
            reduced(co, 1).then_inc(sem("angles"), 1)
            row = lambda r: R[:, r, :]
            dve.wait_ge(sem("mag_ready"), 1)
            dve.wait_ge(sem("sines"), 1)
            step(tt(row(11), row(32), row(16), ALU.mult))
            step(tt(row(12), row(32), row(24), ALU.mult))
            step(V.tensor_scalar(row(11), row(11), -1.0, None, ALU.add))
            step(tt(row(13), row(0), row(0), ALU.mult))
            step(tt(row(14), row(1), row(1), ALU.mult))
            step(tt(row(13), row(13), row(14), ALU.add))
            step(V.reciprocal(row(13), row(13)))
            step(tt(row(14), row(11), row(0), ALU.mult))
            step(tt(row(15), row(12), row(1), ALU.mult))
            step(tt(row(14), row(14), row(15), ALU.add))
            step(tt(row(33), row(14), row(13), ALU.mult))
            step(tt(row(14), row(12), row(0), ALU.mult))
            step(tt(row(15), row(11), row(1), ALU.mult))
            step(tt(row(14), row(14), row(15), ALU.subtract))
            tt(row(34), row(14), row(13), ALU.mult).then_inc(sem("ssm_rows"), 1)
            dve.wait_ge(sem("vecs_psum"), 1)
            step(V.tensor_copy(vecs[:], PS[:, 4, 0:49]))
            step(V.tensor_copy(adab[:], PS[:, 4, 64:160]))
            dve.wait_ge(sem("siluc_psum"), 1)
            V.tensor_copy(siluc[:], PS[:, 5, 0:128].rearrange("p (k c) -> p k c", k=KT)[:, :, 0:NC])\
                .then_inc(sem("siluc_ready"), 1)
            g = 0
            for i in range(TT):
                for half in range(2):
                    dve.wait_ge(sem("x_psum"), g + 1)
                    V.tensor_copy(xT[:, half * 4:half * 4 + 4, i * P:i * P + TOK[i]],
                                  PS[:, 2 * (i % 2) + half, :].rearrange("p (k t) -> p k t", k=4)[:, :, 0:TOK[i]])\
                        .then_inc(sem("x_turned"), 1)
                    g += 1
            def mod_bias(q, bank):
                dve.wait_ge(sem("mod_turn_psum"), q + 1)
                tt(mod[:, 4 * q:4 * q + 4, :], PS[:, bank, 0:4 * NC].rearrange("p (a c) -> p a c", a=4),
                   bc(adab[:, 4 * q:4 * q + 4], 2, NC), ALU.add).then_inc(sem("mod_ready"), 1)

            for q in pairs0:
                mod_bias(q, 6)
            dve.wait_ge(sem("ssm_psum"), 1)
            V.tensor_copy(sT[:, 0:10, :], PS[:, 4, 0:320].rearrange("p (m g) -> p m g", g=GP))
            step(V.tensor_copy(sT[:, 10:19, :], PS[:, 5, 0:288].rearrange("p (m g) -> p m g", g=GP)))
            dve.wait_ge(sem("x0_psum"), 1)
            for a in range(2):
                last = V.tensor_copy(x0T[a].rearrange("p b g -> p (b g)"), PS[:, 6, a * 256:a * 256 + 256])
            step(last)
            for a in range(2):
                last = tt(lamT[a], sT[:, 16, :], sT[:, 8 * a, :], ALU.mult)
            step(last)
            lr, li = (bc(lamT[a], 1, NB) for a in range(2))
            step(tt(addT[0], x0T[0], lr, ALU.mult))
            step(tt(addT[1], x0T[1], li, ALU.mult))
            step(tt(addT[0], addT[0], addT[1], ALU.subtract))
            step(tt(x0T[1], x0T[1], lr, ALU.mult))
            step(tt(addT[1], x0T[0], li, ALU.mult))
            step(tt(addT[1], addT[1], x0T[1], ALU.add))
            dve.wait_ge(sem("ld_bc"), 96)
            cr, ci = (bc(sT[:, 17 + a, :], 2, 16) for a in range(2))
            dve.wait_ge(sem("bexp_zero"), 2)
            for a, (f, g2, op) in enumerate(((0, 1, ALU.subtract), (1, 0, ALU.add))):
                step(tt(t512[0], bnat[f], cr, ALU.mult))
                step(tt(t512[1], bnat[g2], ci, ALU.mult))
                for half in range(2):
                    p0 = 64 * half
                    o = bexp[a].rearrange("p k (j u c) -> p (k j) u c", j=4, u=2)[p0:p0 + 64, :, half, :]
                    last = tt(o, t512[0][p0:p0 + 64], t512[1][p0:p0 + 64], op)
                step(last)
            for a in range(2):
                for u in range(2):
                    last = V.tensor_scalar(cexp[a][:, :, 64 * u:64 * u + 64], cnat[a], const[:, C_PAR + u:C_PAR + u + 1],
                                           -1.0 if a else 1.0, ALU.mult, ALU.mult)
            last.then_inc(sem("mats_made"), 1)
            g = 0
            for dst in (bbt[0], bbt[1], cct[0], cct[1]):
                for half in range(2):
                    dve.wait_ge(sem("mats_psum"), g + 1)
                    V.tensor_copy(dst[:, half * 4:half * 4 + 4, :],
                                  PS[:, (2, 3, 4, 7)[g % 4], :].rearrange("p (k n) -> p k n", k=4))\
                        .then_inc(sem("mats_turned"), 1)
                    g += 1
            dve.wait_ge(sem("mod_ready"), 4)
            norm((vecs[:, 0:8], layer_mod(0, 1)), layer_mod(0, 0))
            dve.wait_ge(sem("softplus_ready"), 1)
            step(V.scalar_tensor_tensor(hf, hf, 0.0, hb, ALU.min, ALU.subtract))
            for h in range(H):
                last = V.tensor_tensor_scan(hb[:, h, :], const[:, C_KEEP:C_KEEP + T], hf[:, h, :], 0.0, ALU.mult, ALU.add)
            last.then_inc(sem("b_ready"), 1)
            dve.wait_ge(sem("expb_ready"), 1)
            tt(hf, hf, hq, ALU.mult).then_inc(sem("qfull_ready"), 1)
            a = 1
            dve.wait_ge(sem("decays_ready"), a)
            tt(hT[:], hT[:], hk, ALU.mult).then_inc(sem("kend_ready"), 1)
            g = 0
            for i in range(TT):
                for half in range(2):
                    dve.wait_ge(sem("kt_psum"), g + 1)
                    V.tensor_copy(hkt[0:TOK[i], i, half * 512:half * 512 + 512], PS[0:TOK[i], 6 + g % 2, :])\
                        .then_inc(sem("kt_ready"), 1)
                    g += 1
            for u, (i, kind, m) in enumerate(units):
                n = TOK[i]
                nb = n // BLK
                if kind == "J" and m == 1:
                    a += 1
                    dve.wait_ge(sem("decays_ready"), a)
                    tt(qblk[:, :, BLK:], qblk[:, :, BLK:], hq[:, :, i * P + BLK:i * P + P], ALU.mult)\
                        .then_inc(sem("qblk_ready"), 1)
                a += 1
                dve.wait_ge(sem("decays_ready"), a)
                if kind == "J":
                    e = ea[u % 3][:, :, 0:BLK * m]
                    last = tt(e, e, hk[:, :, i * P:i * P + BLK * m], ALU.mult)
                else:
                    e = ea[u % 3][:, :, 0:n]
                    last = V.scalar_tensor_tensor(e, e, 1.0, hk[:, :, i * P:i * P + n], ALU.min, ALU.mult)
                last.then_inc(sem("keys_ready"), 1)
                if u > mod_lag_bias and (u - mod_lag_bias) % 2 and (u - mod_lag_bias) // 2 < len(pairs1):
                    mod_bias(pairs1[(u - mod_lag_bias) // 2], 4)
                if u in sample_at:
                    h = sample_at[u]
                    sl = st0[:, :, h, :]
                    if h == 0:
                        dve.wait_ge(sem("o_psum"), 1)
                        dve.wait_ge(sem("dec_ready"), 2)
                    step(tt(sl, sl, bc(decs[:, h, :], 2, P), ALU.mult))
                    dve.wait_ge(sem("state0_psum"), 1 + h)
                    tt(sl, sl, PS[:, 6:8, :].rearrange("p c (b e) -> p (c b) e", b=4), ALU.add).then_inc(sem("state0_new"), 1)
                if u + 1 != unit_end[i]:
                    continue
                dve.wait_ge(sem("keys_used"), u + 1)
                if i != 2:
                    dve.wait_ge(sem("o_psum"), o_part[i])
                nbank = BLK * H * nb // 512
                for hh in range(H):
                    own = PS[0:n, 2:2 + nbank, :].rearrange("p c x -> p (c x)").rearrange("p (r h b) -> p h b r", r=BLK, h=H)[:, hh]
                    out = scores[0:n, hh, 0:n].rearrange("p (b r) -> p b r", r=BLK)
                    mask = const[0:n, C_CAUSAL:C_CAUSAL + n].rearrange("p (b r) -> p b r", r=BLK)
                    last = tt(out, own, mask, ALU.mult)
                if i == 2:
                    last.then_inc(sem("scores_ready"), 1)
                else:
                    step(last)
                    tt(scores[:, :, :].rearrange("p (c h) t -> p c (h t)", c=2), scores[:, :, :].rearrange("p (c h) t -> p c (h t)", c=2),
                       PS[:, 0:2, :], ALU.add).then_inc(sem("scores_ready"), 1)
                if i == 1:
                    dve.wait_ge(sem("state_psum"), 2)
                    for h in range(H):
                        last = V.scalar_tensor_tensor(st1[:, h, :], st1[:, h, :], decp[:, h:h + 1],
                                                      PS[:, 6 + h // 4, (h % 4) * P:(h % 4 + 1) * P], ALU.mult, ALU.add)
                    last.then_inc(sem("state1_ready"), 1)
            dve.wait_ge(sem("o_root"), 1)
            step(V.reciprocal(hk, hk))
            step(tt(hT[:], hT[:], hk, ALU.mult))
            V.scalar_tensor_tensor(hT[:], hT[:], vecs[:, 48:49], hg, ALU.mult, ALU.mult).then_inc(sem("o_ready"), 1)
            for dt in range(KT):
                dve.wait_ge(sem("hout_psum"), dt + 1)
                residual(PS[:, dt % 4, :], dt, layer_mod(0, 2), sem("hout_read"))
            dve.wait_ge(sem("hout_read"), KT)
            dve.sem_inc(sem("x_ready"), 1)
            norm((vecs[:, 8:16], layer_mod(0, 4)), layer_mod(0, 3))
            dve.sem_inc(sem("fin_credit"), 2)
            with dve.Fori(0, FT // 2) as i:
                for c in range(2):
                    dve.wait_ge(sem("up_psum"), i * 2 + c + 1)
                    dve.wait_ge(sem("silu_ready"), i * 2 + c + 1)
                    tt(midf[:, bass.ds(i * (2 * T) + c * T, T)], acts[:, c, :], PS[:, 2 * c + 1, 0:T], ALU.mult)\
                        .then_inc(sem("fin_credit"), 1)
            dve.wait_ge(sem("fin_credit"), 2 + FT)
            dve.sem_inc(sem("mid_ready"), FT)
            dve.sem_inc(sem("fout_credit"), 2)
            for dt in range(KT):
                dve.wait_ge(sem("fout_psum"), dt + 1)
                residual(PS[:, dt % 2, :], dt, layer_mod(0, 5), sem("fout_credit"))
            dve.wait_ge(sem("fout_credit"), 2 + KT)
            dve.sem_inc(sem("x_ready"), 1)
            norm((vecs[:, 16:24], layer_mod(1, 1)), layer_mod(1, 0))
            dve.wait_ge(sem("tables_ready"), 1)
            NW = GP // 2
            for w in range(NW):
                v, z, u = vb[w % 2], zb, ub[w % 2]
                dve.wait_ge(sem("bu_read"), 4 * w + 4)
                if w >= 2:
                    dve.wait_ge(sem("xs_used"), w - 1)
                    dve.wait_ge(sem("fin_states"), w - 1)
                for a in range(2):
                    first = u[a][:, :, NP::NS]
                    last = tt(first, first, addT[a][:, :, 2 * w:2 * w + 2].rearrange("p b g -> p g b"), ALU.add)
                step(last)
                rotate(step, tt, v, u, wd, w, ALU.add, ALU.subtract, (1,))
                dve.sem_inc(sem("u_used"), 1)
                dve.wait_ge(sem("v_ready"), w + 1)
                for j in range(2):
                    gp = 2 * w + j
                    for b in range(2):
                        V.tensor_tensor_scan(z[b][:, j, 0:NP], sT[:, 16, gp:gp + 1].to_broadcast([P, NP]), v[b][:, j, 0:NP],
                                             0.0, ALU.mult, ALU.add)
                        last = V.tensor_tensor_scan(z[b][:, j, NP:T], magk[:, gp, :], v[b][:, j, NP:T], 0.0, ALU.mult, ALU.add)
                step(last)
                rotate(step, tt, v, z, wd, w, ALU.subtract, ALU.add)
                dve.sem_inc(sem("xs_ready"), 1)
                if w > 2 and w % 2:
                    mod_bias(pairs2[w // 2 - 1], 7)
                if w % 2 == 1 and w > 2:
                    k = w // 2 - 1
                    dve.wait_ge(sem("xs_used"), w - 1)
                    V.scalar_tensor_tensor(hT[:, k, :], hT[:, k, :], vecs[:, 40 + k:41 + k], PS[:, 4 + k % 2, 0:T],
                                           ALU.mult, ALU.add).then_inc(sem("y5_read"), 1)
            mod_bias(pairs2[-1], 7)
            k = KT - 1
            dve.wait_ge(sem("xs_used"), NW)
            V.scalar_tensor_tensor(hT[:, k, :], hT[:, k, :], vecs[:, 40 + k:41 + k], PS[:, 4 + k % 2, 0:T],
                                   ALU.mult, ALU.add).then_inc(sem("y5_read"), 1)
            dve.sem_inc(sem("glu_credit"), 2)
            for dt in range(KT):
                dve.wait_ge(sem("glu_a_psum"), dt + 1)
                dve.wait_ge(sem("sigmoid_ready"), dt + 1)
                if dt:
                    dve.wait_ge(sem("glu_credit"), 2 + dt)
                step(tt(gated[:], acts[:, dt % 2, :], PS[:, 2 * (dt % 2), 0:T], ALU.mult))
                residual(gated[:], dt, layer_mod(1, 2), sem("glu_credit"))
            dve.wait_ge(sem("glu_credit"), 2 + KT)
            dve.sem_inc(sem("x_ready"), 1)
            norm((vecs[:, 24:32], layer_mod(1, 4)), layer_mod(1, 3))
            step(V.memset(rt, 0.0))
            step(V.memset(macc, 0.0))
            L, one, chosen, gate, place, l2, t1, t2, two_ = (rt[:, r] for r in range(9))
            dve.wait_ge(sem("logits"), 1)
            for i in range(TT):
                last = V.tensor_copy(L[0:TOK[i], i, :], PS[0:TOK[i], 4, 16 * i:16 * i + NE])
            step(last)
            step(V.tensor_scalar(rt[:, 9, 0, :], const[:, C_IOTA:C_IOTA + NE], -1.0, float(NE), ALU.mult, ALU.add))
            rank = bc(rt[:, 9, 0, :], 1, TT)

            def best(out, lg, m, mm):
                step(V.tensor_reduce(rm[:, m, :], lg, AX.X, ALU.max))
                step(tt(t1, lg, bc(rm[:, m, :], 2, NE), ALU.is_equal))
                step(tt(t1, t1, rank, ALU.mult))
                step(V.tensor_reduce(rm[:, mm, :], t1, AX.X, ALU.max))
                step(tt(out, t1, bc(rm[:, mm, :], 2, NE), ALU.is_equal))

            best(one, L, 0, 1)
            step(V.scalar_tensor_tensor(l2, one, -3.0e38, L, ALU.mult, ALU.add))
            best(two_, l2, 2, 3)
            tt(chosen, one, two_, ALU.add).then_inc(sem("chosen"), 1)
            dve.wait_ge(sem("chosen"), 1)
            tt(rm[:, 4, :], rm[:, 2, :], rm[:, 0, :], ALU.subtract).then_inc(sem("second_less_first"), 1)
            dve.wait_ge(sem("second_exp"), 1)
            step(V.tensor_scalar(rm[:, 6, :], rm[:, 5, :], 1.0, None, ALU.add))
            step(V.reciprocal(rm[:, 6, :], rm[:, 6, :]))
            step(tt(rm[:, 7, :], rm[:, 6, :], rm[:, 5, :], ALU.mult))
            step(tt(t1, one, bc(rm[:, 6, :], 2, NE), ALU.mult))
            step(tt(t2, two_, bc(rm[:, 7, :], 2, NE), ALU.mult))
            step(tt(gate, t1, t2, ALU.add))
            dve.wait_ge(sem("places"), 1)
            for i in range(TT):
                last = V.tensor_copy(place[0:TOK[i], i, :], PS[0:TOK[i], 5, 16 * i:16 * i + NE])
            step(last)
            step(V.scalar_tensor_tensor(place, place, 1.0, chosen, ALU.add, ALU.mult))
            step(V.tensor_scalar(place, place, -1.0, None, ALU.add))
            cnt = rt[0:1, 10, 0, 0:1]
            step(V.tensor_reduce(cnt, PS[0:1, 5, 64:64 + NE], AX.X, ALU.max))
            step(V.tensor_scalar(rt[0:1, 11, 0, 0:1], cnt, float(CAP), None, ALU.is_gt))
            for k in range(2, PASSES):
                step(V.scalar_tensor_tensor(rt[0:1, 11, 0, 0:1], cnt, float(CAP * k), rt[0:1, 11, 0, 0:1], ALU.is_gt, ALU.add))
            V.tensor_scalar(npass[:], rt[0:1, 11, 0, 0:1], 1.0, None, ALU.add).then_inc(sem("passes_known"), 1)
            dve.wait_ge(sem("passes_known"), 1)
            dve.sem_inc(sem("emid_done"), NST)
            dve.sem_inc(sem("scatter_read"), KT)
            n_pass = dve.value_load(npass[0:1, 0:1], min_val=1, max_val=PASSES)
            placef = place.rearrange("p i e -> p (i e)")
            gatef = gate.rearrange("p i e -> p (i e)")
            with dve.Fori(0, n_pass) as ps:
                with dve.Fori(0, NE) as e:
                    it = ps * NE + e
                    for i in range(TT):
                        n = TOK[i]
                        at = bass.ds(e + i * NE, 1)
                        V.tensor_scalar(pick[0:n, i, :], const[0:n, C_IOTA:C_IOTA + CAP], placef[0:n, at], None, ALU.is_equal)
                        last = V.tensor_scalar(pickg[0:n, i, :], const[0:n, C_IOTA:C_IOTA + CAP], placef[0:n, at],
                                               gatef[0:n, at], ALU.is_equal, ALU.mult)
                    last.then_inc(sem("pick_ready"), 1)
                    for s in range(NST):
                        dve.wait_ge(sem("sig_ready"), it * NST + s + 1)
                        tt(emid[:, 2 * s:2 * s + 2, :].rearrange("p c n -> p (c n)"), sig[:, s % 2, :],
                           PS[:, s % 3, 2 * CAP:4 * CAP], ALU.mult).then_inc(sem("emid_done"), 1)
                    for dt in range(KT):
                        dve.wait_ge(sem("scatter_psum"), it * KT + dt + 1)
                        tt(macc[:, dt, :], macc[:, dt, :], PS[:, 6 + dt % 2, 0:T], ALU.add).then_inc(sem("scatter_read"), 1)
                    dve.wait_ge(sem("scatter_read"), it * KT + 2 * KT)
                V.tensor_scalar(placef, placef, -float(CAP), None, ALU.add).then_inc(sem("pass_done"), 1)
                dve.wait_ge(sem("pass_done"), ps + 1)
            for dt in range(KT):
                last = residual(macc[:, dt, :], dt, layer_mod(1, 5), sem("x_macc"))
            dve.wait_ge(sem("x_macc"), KT)
            dve.sem_inc(sem("x_ready"), 1)
            norm((vecs[:, 32:40], None), None)
            g = 0
            for i in range(TT):
                for half in range(2):
                    dve.wait_ge(sem("y_out_psum"), g + 1)
                    V.tensor_copy(yout[0:TOK[i], i, half * 512:half * 512 + 512], PS[0:TOK[i], g % 4, :])\
                        .then_inc(sem("y_ready"), 1)
                    g += 1

        @block.gpsimd
        def _(pool):
            G = nc.gpsimd
            step = Steps(pool, sem("pool_step"))

            def tt(out, a, b, op):
                return G.tensor_tensor(out, a, b, op)

            for a in range(2):
                G.memset(bexp[a], 0.0).then_inc(sem("bexp_zero"), 1)
            pool.wait_ge(sem("mats_turned"), 8)
            pool.dma_start(prep, kept).then_inc(sem("prep_stored"), 16)
            pool.wait_ge(sem("b_ready"), 1)
            pool.wait_ge(sem("zeros"), 1)
            for i in range(2):
                tt(hT[:, :, i * P:i * P + P], bc(hb[:, :, i * P + P - 1], 2, P), hb[:, :, i * P:i * P + P], ALU.subtract)
            sv = lambda ap: ap[:, :, NP:T].rearrange("p h (b t) -> p h b t", b=NB)
            tt(sv(hT[:]), bc(sv(hb)[:, :, :, NS - 1], 3, NS), sv(hb), ALU.subtract).then_inc(sem("args_ready"), 1)
            for u, (i, kind, m) in enumerate(units):
                n = TOK[i]
                if kind == "J" and m == 1:
                    if i == 1:
                        pool.wait_ge(sem("keys_used"), unit_end[0])
                    q = hb[:, :, i * P + BLK:i * P + P].rearrange("p h (b r) -> p h b r", r=BLK)
                    tt(qblk[:, :, BLK:].rearrange("p h (b r) -> p h b r", r=BLK), q,
                       bc(hb[:, :, i * P + BLK - 1:i * P + P - 1:BLK], 3, BLK), ALU.subtract).then_inc(sem("args_ready"), 1)
                if u >= 3:
                    pool.wait_ge(sem("keys_used"), u - 2)
                if kind == "J":
                    last = tt(ea[u % 3][:, :, 0:BLK * m], bc(hb[:, :, i * P + BLK * m - 1], 2, BLK * m),
                              hb[:, :, i * P:i * P + BLK * m], ALU.subtract)
                else:
                    k = hb[:, :, i * P:i * P + n].rearrange("p h (b r) -> p h b r", r=BLK)
                    last = tt(ea[u % 3][:, :, 0:n].rearrange("p h (b r) -> p h b r", r=BLK),
                              bc(k[:, :, :, m], 3, BLK), k, ALU.subtract)
                last.then_inc(sem("args_ready"), 1)
                if u in sample_at:
                    h = sample_at[u]
                    if h:
                        pool.wait_ge(sem("state0_psum"), h)
                    tt(vmask[0:64], bc(hv[0:64, 2, h * P:(h + 1) * P], 1, NB), bc(const[0:64, C_SAMPLE:C_SAMPLE + NB], 2, P),
                       ALU.mult).then_inc(sem("vmask_ready"), 1)
            pool.wait_ge(sem("hgrn_out"), 32)
            pool.wait_ge(sem("o_ready"), 1)
            tt(magk, bc(sT[:, 16, :], 2, NB * NS), bc(const[:, C_KEEP + NP:C_KEEP + T], 1, GP), ALU.mult)
            G.memset(rot_c[:, :, 0:1], 1.0)
            step(G.memset(rot_s[:, :, 0:1], 0.0))
            for k in range(8):
                n = 2 ** k
                for c in range(0, n, 32):
                    m = min(n, 32)
                    pc, psn = bc(sT[:, k, :], 2, m), bc(sT[:, 8 + k, :], 2, m)
                    c0, s0 = rot_c[:, :, c:c + m], rot_s[:, :, c:c + m]
                    c1, s1 = rot_c[:, :, n + c:n + c + m], rot_s[:, :, n + c:n + c + m]
                    ta, tb = rtmp[0][:, :, 0:m], rtmp[1][:, :, 0:m]
                    step(tt(c1, c0, pc, ALU.mult))
                    step(tt(ta, s0, psn, ALU.mult))
                    step(tt(s1, c0, psn, ALU.mult))
                    step(tt(tb, s0, pc, ALU.mult))
                    step(tt(c1, c1, ta, ALU.subtract))
                    step(tt(s1, s1, tb, ALU.add))
            pool.sem_inc(sem("tables_ready"), 1)
            pool.wait_ge(sem("ld_kept"), 16)
            NW = GP // 2
            for w in range(NW):
                u = ub[w % 2]
                pool.wait_ge(sem("bu_read"), 4 * w + 4)
                if w >= 2:
                    pool.wait_ge(sem("xs_used"), w - 1)
                    pool.wait_ge(sem("fin_states"), w - 1)
                rotate(step, tt, vb[w % 2], u, wp, w, ALU.add, ALU.subtract, (0,))
                pool.sem_inc(sem("v_ready"), 1)


def constants(np):
    c = np.zeros((P, C_W), np.float32)
    s = np.arange(P)[:, None]
    t = np.arange(P)[None, :]
    c[:, C_ID:C_ID + P] = s == t
    c[:, C_BEFORE:C_BEFORE + P] = s < t
    c[:, C_ONE:C_ONE + P] = 1
    c[:, C_CAUSAL:C_CAUSAL + P] = (s // BLK == t // BLK) & (s <= t)
    c[:, C_SAMPLE:C_SAMPLE + NB] = s // NS == t[:, 0:NB]
    keep = np.ones(T, np.float32)
    keep[[0, P]] = 0
    keep[NP::NS] = 0
    c[:, C_KEEP:C_KEEP + T] = keep
    c[:, C_PAR:C_PAR + 2] = (s // 16) % 2 == t[:, 0:2]
    c[:, C_IOTA:C_IOTA + P] = t
    return c


_INS = ["x_prompt", "x_sample", "state_hgrn", "state_ssm_re", "state_ssm_im", "c_prompt", "c_sample", "norm_w",
        "ada_w", "ada_b", "hgrn_w_in", "hgrn_gnorm", "hgrn_w_out", "ssm_a_re", "ssm_a_im",
        "ssm_log_dt", "ssm_b_re", "ssm_b_im", "ssm_c_re", "ssm_c_im", "ssm_d", "ssm_w_glu", "ffn_w_in", "ffn_w_out",
        "moe_w_router", "moe_b_router", "moe_w_in", "moe_w_out", "final_norm_w"]
_OUTS = [(1, NP, D), (NB, NS, D), (1, 1, H, P, P), (1, 1, 64, 64), (1, 1, 64, 64), (1, NB, H, P, P), (1, NB, 64, 64),
         (1, NB, 64, 64)]


def kernel(**inputs):
    import numpy as np
    from concourse import bacc
    from concourse.bass_utils import run_bass_kernel_spmd

    nc = bacc.Bacc("TRN2", target_bir_lowering=False, num_devices=1)
    arrays, ins = {}, {}
    for name in _INS:
        arrays[f"in_{name}"] = np.ascontiguousarray(inputs[name])
    arrays["in_constants"] = constants(np)
    for name in [*_INS, "constants"]:
        ins[name] = nc.dram_tensor(f"in_{name}", arrays[f"in_{name}"].shape, F32, kind="ExternalInput").ap()
    outs = [nc.dram_tensor(f"out_{i}", shape, F32, kind="ExternalOutput").ap() for i, shape in enumerate(_OUTS)]
    prep = nc.dram_tensor("s5_prep", (P, 5120), F32).ap()
    trunk(nc, ins, outs, prep)
    r = run_bass_kernel_spmd(nc, [arrays], core_ids=[0])
    return tuple(r.results[0][f"out_{i}"] for i in range(len(_OUTS)))
```

```python
from contextlib import ExitStack

import concourse.bass as bass
from concourse import mybir

F32 = mybir.dt.float32
I32 = mybir.dt.int32
BF16 = mybir.dt.bfloat16
F32R = mybir.dt.float32r
ALU = mybir.AluOpType
ACT = mybir.ActivationFunctionType
AX = mybir.AxisListType

P = 128
D = 1024
KT = D // P
NP = 256
NB = 8
NS = 8
T = NP + NB * NS
TT = 3
TOK = [P, P, NB * NS]
NC = 1 + NB
H = 8
LEVELS = (64, 32, 16, 8, 4, 2, 1, 0)
FF = 2816
FT = FF // P
NE = 8
GP = 32
EPS = 1e-6
SLAB = 2048
RING = 4
XRING = 9
HRING = 3
CAP = 112
PASSES = -(-T // CAP)
TWO_PI = 6.283185307179586
PI_A, PI_B, PI_C = 6.28125, 0.0019350051879882812, 3.0199157e-07
ROUND = 12582912.0

C_ID, C_BEFORE, C_ONE = (128 * i for i in range(3))
C_SAMPLE = 384
C_KEEP = 392
C_PAR = 712
C_IOTA = 714
C_W = 842


class Steps:

    def __init__(self, eng, done, base=0):
        self.eng, self.done, self.base, self.n = eng, done, base, 0

    def __call__(self, ins):
        self.n += 1
        ins.then_inc(self.done, 1)
        self.eng.wait_ge(self.done, self.base + self.n)


def trunk(nc, I, outs, prep):
    with ExitStack() as ctx:
        def sb(name, shape, dt=F32):
            return ctx.enter_context(nc.sbuf_tensor(name, shape, dt))

        sems = {}

        def sem(name):
            if name not in sems:
                sems[name] = ctx.enter_context(nc.semaphore(name))
            return sems[name]

        PS = ctx.enter_context(nc.psum_tensor("PS", [P, 8, 512], F32))

        const = sb("const", [P, C_W])
        xT = sb("xT", [P, KT, T])
        hT = sb("hT", [P, KT, T])
        mod = sb("mod", [P, 96, NC])
        siluc = sb("siluc", [P, KT, NC])
        vecs = sb("vecs", [P, 49])
        adab = sb("adab", [P, 96])
        scale_a = sb("scale_a", [P, KT, NC])
        rstd = sb("rstd", [P, T])
        root = sb("root", [P, T])
        gtmp = sb("gtmp", [P, KT * NB * NS])
        lmask = gtmp[:].rearrange("p (l t) -> p l t", t=P)
        work = sb("work", [P, 1024])
        acts = work[:, 0:2 * T].rearrange("p (s t) -> p s t", s=2)
        gated = work[:, 2 * T:3 * T]
        modrow = work[0:NC, :].rearrange("p (s n) -> p s n", s=2)
        sT = sb("sT", [P, 19, GP])
        ring = sb("ring", [P, RING, SLAB])
        zero16 = sb("zero16", [P, 512], BF16)
        wr = sb("wr", [P, KT, NE])
        br = sb("br", [1, NE])
        epst = sb("epst", [P, 1])
        npass = sb("npass", [1, 1], I32)
        AR = 34380
        with nc.sbuf_tensor("arena", [P, AR], F32) as arena:
            pass
        NEXACT = 2 * HRING * SLAB + 2 * KT * CAP + 8 * CAP
        exact = sb("exact", [P, NEXACT], F32R)

        def ar(off, *shape, parts=P):
            n = 1
            for k in shape:
                n *= k
            assert off + n <= AR, (off + n, AR)
            v = arena[0:parts, off:off + n]
            if len(shape) == 1:
                return v
            names = "abcd"[:len(shape)]
            return v.rearrange(f"p ({' '.join(names)}) -> p {' '.join(names)}", **dict(zip(names, shape)))

        ident = const[:, C_ID:C_ID + P]

        rot_c = ar(7168, GP, NP)
        rot_s = ar(7168 + GP * NP, GP, NP)
        keep5 = 7168 + 2 * GP * NP
        bbt = [ar(keep5 + 1024 * i, KT, P) for i in range(2)]
        cct = [ar(keep5 + 2048 + 1024 * i, KT, P) for i in range(2)]
        x0T = [ar(keep5 + 4096 + 256 * i, NB, GP) for i in range(2)]
        addT = [ar(keep5 + 4608 + 256 * i, NB, GP) for i in range(2)]
        KEPT = 5120
        kept = ar(keep5, KEPT)
        magk = ar(keep5 + KEPT, GP, NB * NS)
        s5w = keep5 + KEPT + GP * NB * NS
        bnat = [ar(keep5 + KEPT + 512 * i, GP, 16) for i in range(2)]
        cnat = [ar(keep5 + KEPT + 1024 + 512 * i, KT, 64) for i in range(2)]
        bexp = [ar(keep5 + KEPT + 2048 + 1024 * i, KT, P) for i in range(2)]
        cexp = [ar(20700 + 1024 * i, KT, P) for i in range(2)]
        x0n = [ar(keep5 + KEPT + 4096 + 256 * i, 2, P) for i in range(2)]
        xin = ar(8192, TT, D)
        crow = ar(12288, D, parts=NC)
        rowA = ar(13312, P, parts=49)
        rowB = ar(13440, P, parts=96)
        ssr = ar(13600, 46, P, parts=GP)
        t512 = [ar(19500 + 512 * i, GP, 16) for i in range(2)]
        lamT = [ar(20600 + 32 * i, GP) for i in range(2)]
        ub = [[ar(1280 * s + 640 * a, 2, T) for a in range(2)] for s in range(2)]
        vb = [[ar(2560 + 1280 * s + 640 * a, 2, T) for a in range(2)] for s in range(2)]
        zb = [ar(5120 + 640 * a, 2, T) for a in range(2)]
        fin = [ar(6400 + 288 * i, 9, GP) for i in range(2)]
        wp = [ar(s5w + 640 * a, 2, T) for a in range(2)]
        wd = [ar(s5w + 1280 + 640 * a, 2, T) for a in range(2)]
        fout = ar(s5w + 2560, 6, P)
        rtmp = [ar(s5w, GP, 32), ar(s5w + 1024, GP, 32)]
        W8 = KT * T
        hq, hg, hk, hf, hb = (ar(W8 * i, H, T) for i in range(5))
        hbflat = ar(W8 * 4, W8)
        o0 = 5 * W8
        hv = ar(o0, TT, D)
        hkt = ar(o0 + 3072, TT, D)
        ekq = [ar(o0 + 6144 + 1024 * i, H, P) for i in range(4)]
        scores = ar(o0 + 10240, H, P)
        st1 = ar(o0 + 11264, H, P)
        vmask = ar(o0 + 12288, NB, P)
        st0 = ar(o0 + 13312, NB, H, P)
        decp = ar(o0 + 21504, H)
        decs = ar(o0 + 21512, H, NB)
        mid = ar(0, FT, T)
        midf = ar(0, FT * T)
        wparts = [exact[:, x * HRING * SLAB:(x + 1) * HRING * SLAB].rearrange("p (r n) -> p r n", r=HRING) for x in range(2)]
        x0 = 2 * HRING * SLAB
        hexp = [exact[:, x0 + KT * CAP * x:x0 + KT * CAP * (x + 1)].rearrange("p (k n) -> p k n", k=KT) for x in range(2)]
        x0 += 2 * KT * CAP
        emid = [[exact[:, x0 + 2 * CAP * (2 * b + x):x0 + 2 * CAP * (2 * b + x + 1)] for x in range(2)] for b in range(2)]
        NX = XRING - RING
        xring = ar(NEXACT, NX, SLAB)
        x0 = NEXACT + NX * SLAB
        htok = ar(x0, TT, D)
        x0 += TT * D
        sig = ar(x0, 2, 256)
        egated = ar(x0 + 512, 2, 256)
        x0 += 1024
        pick = ar(x0, TT, CAP)
        pickg = ar(x0 + TT * CAP, TT, CAP)
        x0 += 2 * TT * CAP
        pickT = ar(x0, T)
        yexp = ar(x0 + T, D)
        macc = ar(x0 + T + D, KT, T)
        x0 += T + D + W8
        rt = ar(x0, 12, TT, NE)
        rm = ar(x0 + 12 * TT * NE, 8, TT)
        x0 += 12 * TT * NE + 8 * TT
        xplace = ar(x0, NE + 1, TT)
        xgate = ar(x0 + (NE + 1) * TT, NE + 1, TT)
        yout = htok

        def bc(ap, axis, n):
            return ap.unsqueeze(axis).to_broadcast(list(ap.shape[:axis]) + [n] + list(ap.shape[axis:]))

        def layer_mod(layer, part):
            a = layer * 48 + part * 8
            return mod[:, a:a + 8, :]

        n_mod = (8, 24, 16)
        s_mod0 = 0
        s_hin = s_mod0 + n_mod[0]
        s_mod1 = s_hin + 16
        s_hout = s_mod1 + n_mod[1]
        s_fin = s_hout + 4
        s_fout = s_fin + 22
        s_mod2 = s_fout + 16
        s_glu = s_mod2 + n_mod[2]
        slab_in = [sem(f"slab_in{i}") for i in range(RING)]
        slab_credit = sem("slab_credit")

        NST = FT // 2
        order = []
        for s in range(NST):
            order += [("g", s), ("u", s)] + ([("o", s - 2)] if s >= 2 else [])
        order += [("o", NST - 2), ("o", NST - 1)]
        NSL = len(order)
        assert NSL % HRING == 0
        uses = [sum(1 for j in range(NSL) if j % XRING == q) for q in range(XRING)]
        eindex = {k: j for j, k in enumerate(order)}

        def eslot(j):
            return (j % NSL) % XRING

        def eslab(j):
            return xring[:, eslot(j), :] if eslot(j) < NX else ring[:, eslot(j) - NX, :]

        def arrivals(j):
            return (j % NSL) // XRING + 1 + (uses[eslot(j)] if j >= NSL else 0)

        def f32(ap):
            return ap.bitcast(F32)

        units = [(i, L) for i in (2, 0, 1) for L in LEVELS if i < 2 or L < NS]
        tiles = (2, 0, 1)
        decayed = [u for u, (i, L) in enumerate(units) if L]
        masked = [u for u, (i, L) in enumerate(units) if L < 16]
        unit_end = {i: max(u for u, x in enumerate(units) if x[0] == i) + 1 for i in range(TT)}
        o_part = {2: 0, 0: 1, 1: 3}
        sample_at = {unit_end[2] + h: h for h in range(H)}
        free_units = [u for u in range(len(units)) if u + 1 not in unit_end.values()]
        pairs0, pairs1, pairs2 = range(0, 4), range(4, 16), range(16, 24)
        mod_at = {u: q for u, q in zip(free_units, pairs1)}
        turn_at = {u: q for u, q in zip(free_units[1:], pairs1)}
        turned_by = lambda u: len(pairs0) + sum(1 for x in turn_at if x <= u)

        def finals(eng, A, w):
            eng.wait_ge(sem("xs_ready"), w + 1)
            for a in range(2):
                v = vb[w % 2][a]
                A(fin[a][:, 0, 2 * w:2 * w + 2], v[:, :, NP - 1], ACT.Copy)
                last = A(fin[a][:, 1:9, 2 * w:2 * w + 2].rearrange("p b j -> p j b"), v[:, :, NP + NS - 1::NS], ACT.Copy)
            last.then_inc(sem("fin_states"), 1)

        def rotate(step, tt, dst, src, tmp, w, op_re, op_im, which=(0, 1)):
            gs = slice(2 * w, 2 * w + 2)

            def parts(x):
                s = x[:, :, NP:T].rearrange("p j (b t) -> p j b t", b=NB)
                return [x[:, :, 0:NP], s]

            tabs = [[tb[:, gs, :], bc(tb[:, gs, 0:NS], 2, NB)] for tb in (rot_c, rot_s)]
            sums = []
            for q in which:
                re, im, t0, t1, dr, di = [parts(x)[q] for x in (*src, *tmp, *dst)]
                c, s = tabs[0][q], tabs[1][q]
                tt(dr, re, c, ALU.mult)
                tt(t0, im, s, ALU.mult)
                tt(di, im, c, ALU.mult)
                last = tt(t1, re, s, ALU.mult)
                sums += [(dr, t0, op_re), (di, t1, op_im)]
            step(last)
            for x, y, op in sums:
                last = tt(x, x, y, op)
            step(last)

        block = ctx.enter_context(nc.Block())

        @block.sync
        def _(sp):
            def put(n, src, dst=None, more=0):
                sp.wait_ge(slab_credit, n + 1 + more)
                if dst is None:
                    dst = ring[:, n % RING, :].rearrange("p (k c) -> p k c", k=KT)
                sp.dma_start(dst, src).then_inc(slab_in[n % RING], 16)

            def load(dst, src, name):
                sp.dma_start(dst, src).then_inc(sem(name), 16)

            load(const[:], I["constants"], "ld_const")
            load(crow[0:1, :], I["c_prompt"], "ld_c")
            load(crow[1:NC, :], I["c_sample"], "ld_c")
            load(rowA[0:32, :], I["norm_w"].rearrange("l s (k p) -> (l s k) p", p=P), "ld_rows")
            load(rowA[32:40, :], I["final_norm_w"].rearrange("(k p) -> k p", p=P), "ld_rows")
            load(rowA[40:48, :], I["ssm_d"].rearrange("l (k p) -> (l k) p", p=P), "ld_rows")
            load(rowA[48:49, :], I["hgrn_gnorm"], "ld_rows")
            load(rowB, I["ada_b"].rearrange("l (k p) -> (l k) p", p=P), "ld_rows")
            load(xin[:, 0:2, :], I["x_prompt"].rearrange("a (i p) d -> p (a i) d", p=P), "ld_x")
            load(xin[0:64, 2, :], I["x_sample"].rearrange("b t d -> (b t) d"), "ld_x")
            for a, nm in enumerate(("ssm_a_re", "ssm_a_im")):
                load(ssr[:, a, :], I[nm].rearrange("l (g u) s -> (l g) (u s)", u=2), "ld_ssm")
            load(ssr[:, 2, 0:2], I["ssm_log_dt"].rearrange("l (g u) -> (l g) u", u=2), "ld_ssm")
            ada = I["ada_w"].rearrange("l (k p) n -> p (l k) n", p=P)
            for j in range(n_mod[0]):
                put(j, ada[:, 0:KT, j * 256:j * 256 + 256])
            for a, nm in enumerate(("ssm_b_re", "ssm_b_im")):
                load(bnat[a], I[nm].rearrange("l (g u) s c -> (u s) (l g) c", u=2), "ld_bc")
            for a, nm in enumerate(("ssm_c_re", "ssm_c_im")):
                load(cnat[a], I[nm].rearrange("l (k g) c s -> (g c) (l k) s", g=8), "ld_bc")
            for a, nm in enumerate(("state_ssm_re", "state_ssm_im")):
                load(x0n[a], I[nm].rearrange("l (i b) (g u) s -> (b g) (l i) (u s)", u=2, i=2), "ld_bc")
            load(gtmp[:], I["level_masks"], "ld_masks")
            load(wr[:], I["moe_w_router"].rearrange("l (k p) e -> p (l k) e", p=P), "ld_router")
            load(br[:], I["moe_b_router"], "ld_router")
            hw = I["hgrn_w_in"].rearrange("l (k p) n -> p (l k) n", p=P)
            n = s_hin
            for sec in (0, 3, 1, 2):
                for j in range(4):
                    put(n, hw[:, :, sec * D + j * 256:sec * D + j * 256 + 256])
                    n += 1
            with sp.Fori(0, 4) as i:
                for j in range(4):
                    put(s_mod1 + j, ada[:, 0:KT, bass.ds(i * 1024 + 2048 + j * 256, 256)], more=i * 4)
            with sp.Fori(0, 2) as i:
                for j in range(4):
                    put(s_mod1 + 16 + j, ada[:, KT:2 * KT, bass.ds(i * 1024 + j * 256, 256)], more=i * 4)
            how = I["hgrn_w_out"].rearrange("l (k p) n -> p (l k) n", p=P)
            for j in range(4):
                put(s_hout + j, how[:, :, j * 256:j * 256 + 256])
            fw = I["ffn_w_in"].rearrange("l (k p) n -> p (l k) n", p=P)
            for m in range(2):
                put(s_fin + m, fw[:, :, m * FF:m * FF + 256])
            sp.wait_ge(sem("state1_ready"), 2)
            sp.dma_start(outs[2].rearrange("l b h d e -> d (l b h) e"), st1).then_inc(sem("hgrn_out"), 16)
            sp.wait_ge(sem("state0_new"), H)
            sp.dma_start(outs[5].rearrange("l b h d e -> d (l b h) e"),
                         st0.rearrange("p b h e -> p (b h) e")).then_inc(sem("hgrn_out"), 16)
            sp.wait_ge(sem("hgrn_out"), 32)
            sp.wait_ge(sem("o_ready"), 1)
            load(kept, prep, "ld_kept")
            with sp.Fori(0, 5) as i:
                for j in range(4):
                    col = (j % 2) * FF + (1 + j // 2) * 256
                    put(s_fin + 2 + j, fw[:, :, bass.ds(i * 512 + col, 256)], more=i * 4)
            fo = I["ffn_w_out"].rearrange("l (k p) n -> p (l k) n", p=P)
            with sp.Fori(0, 4) as i:
                for j in range(4):
                    half = j % 2
                    n = s_fout + j
                    put(n, fo[:, half * 11:half * 11 + 11, bass.ds(i * 256 + (j // 2) * P, P)],
                        ring[:, n % RING, 0:11 * P].rearrange("p (k c) -> p k c", k=11), more=i * 4)
            with sp.Fori(0, 4) as i:
                for j in range(4):
                    put(s_mod2 + j, ada[:, KT:2 * KT, bass.ds(i * 1024 + 2048 + j * 256, 256)], more=i * 4)
            gw = I["ssm_w_glu"].rearrange("l (k p) n -> p (l k) n", p=P)
            with sp.Fori(0, 2) as i:
                for j in range(4):
                    put(s_glu + j, gw[:, :, bass.ds(i * 512 + (j % 2) * D + (j // 2) * 256, 256)], more=i * 4)
            sp.wait_ge(sem("fout_ready"), 1)
            for a in range(2):
                sp.dma_start(outs[3 + a].rearrange("l b (g u) s -> (l b g) (u s)", u=2), fout[0:GP, a, :]).then_inc(sem("s5_out"), 16)
                sp.dma_start(outs[6 + a].rearrange("l (i b) (g u) s -> (b g) (l i) (u s)", i=2, u=2),
                             fout[:, 2 + 2 * a:4 + 2 * a, :]).then_inc(sem("s5_out"), 16)
            wi = I["moe_w_in"].rearrange("l e (k p) n -> p (l e k) n", p=P)
            wo = I["moe_w_out"].rearrange("l e (k p) n -> p (l e k) n", p=P)

            def load_slab(j, e):
                kind, s = order[j % NSL]
                dst = eslab(j)
                if kind == "o":
                    src = wo[:, bass.ds(e * FT + s * 2, 2), :]
                    dst = dst.rearrange("p (k c) -> p k c", k=2)
                else:
                    col = (FF if kind == "u" else 0) + s * 256
                    src = wi[:, bass.ds(e * KT, KT), col:col + 256]
                    dst = dst.rearrange("p (k c) -> p k c", k=KT)
                sp.dma_start(dst, src).then_inc(sem(f"expert_in{eslot(j)}"), 16)

            sp.wait_ge(sem("s5_out"), 64)
            sp.wait_ge(sem("z_ready"), 1)
            for j in range(XRING):
                if j == NX:
                    sp.wait_ge(sem("h_ready"), 4)
                load_slab(j, 0)
            sp.wait_ge(sem("passes_known"), 1)
            n_pass = sp.value_load(npass[0:1, 0:1], min_val=1, max_val=PASSES)

            def load_expert(it, e, following):
                for j in range(XRING, NSL + XRING):
                    former = j - XRING if j < NSL else max(x for x in range(NSL) if eslot(x) == eslot(j))
                    if order[former][0] == "o":
                        sp.wait_ge(sem("expert_credit"), it * NSL + former + 4)
                    else:
                        sp.wait_ge(sem("rest_ready"), it * NSL + former + 1)
                    load_slab(j, e if j < NSL else following)

            with sp.Fori(0, n_pass) as ps:
                with sp.Fori(0, NE - 1) as e:
                    load_expert(ps * NE + e, e, e + 1)
                load_expert(ps * NE + NE - 1, NE - 1, 0)
            filled = [n_pass * (NE * n * 16) + 16 for n in range(max(uses) + 1)]
            for j in range(XRING):
                sp.wait_ge(sem(f"expert_in{j}"), filled[uses[j]])
            sp.wait_ge(sem("y_ready"), 6)
            sp.dma_start(outs[0].rearrange("a (i p) d -> p (a i) d", p=P), yout[:, 0:2, :]).then_inc(sem("stored"), 16)
            sp.dma_start(outs[1].rearrange("b t d -> (b t) d"), yout[0:64, 2, :]).then_inc(sem("stored"), 16)
            sp.wait_ge(sem("stored"), 32)
            sp.wait_ge(sem("s5_out"), 64)

        @block.tensor
        def _(pe):
            def tr(out, in_, k):
                return pe.matmul(out, in_, ident[0:k, 0:k], start=True, stop=True)

            def arrived(n, more=0):
                pe.wait_ge(slab_in[n % RING], (n // RING + 1) * 16 + more * 16)

            pe.sem_inc(slab_credit, RING - 1)
            pe.wait_ge(sem("ld_const"), 16)
            pe.wait_ge(sem("ld_rows"), 80)
            tr(PS[:, 4, 0:49], rowA, 49)
            tr(PS[:, 4, 64:160], rowB, 96).then_inc(sem("vecs_psum"), 1)
            pe.wait_ge(sem("silu_c"), 1)
            for k in range(KT):
                last = tr(PS[:, 5, 16 * k:16 * k + NC], crow[:, k * P:(k + 1) * P], NC)
            last.then_inc(sem("siluc_psum"), 1)
            pe.wait_ge(sem("ld_x"), 32)
            for i in range(TT):
                for half in range(2):
                    if i == 2:
                        pe.wait_ge(sem("x_turned"), half + 1)
                    for k in range(4):
                        kk = half * 4 + k
                        last = tr(PS[:, 2 * (i % 2) + half, k * P:k * P + TOK[i]],
                                  xin[0:TOK[i], i, kk * P:(kk + 1) * P], TOK[i])
                    last.then_inc(sem("x_psum"), 1)
            pe.wait_ge(sem("x_turned"), 6)
            pe.wait_ge(sem("siluc_ready"), 1)

            def mod_rows(q, half, bank):
                n = q * 2 + half
                n += s_mod0 if q in pairs0 else s_mod1 - 8 if q in pairs1 else s_mod2 - 32
                if half == 0 and q:
                    pe.wait_ge(sem("mod_rows_read"), q)
                arrived(n)
                for k in range(KT):
                    last = pe.matmul(PS[0:NC, bank, half * 256:half * 256 + 256], siluc[:, k, :],
                                     ring[:, n % RING, k * 256:k * 256 + 256], start=(k == 0), stop=(k == KT - 1))
                    if k == 0:
                        last.then_inc(slab_credit, 1)
                if half:
                    last.then_inc(sem("mod_rows_psum"), 1)

            def mod_turn(q, bank):
                pe.wait_ge(sem("mod_rows_read"), q + 1)
                if q:
                    pe.wait_ge(sem("mod_ready"), q)
                for c in range(4):
                    last = tr(PS[:, bank, c * NC:(c + 1) * NC], modrow[:, q % 2, c * P:(c + 1) * P], NC)
                last.then_inc(sem("mod_turn_psum"), 1)

            for q in pairs0:
                mod_rows(q, 0, q % 2)
                mod_rows(q, 1, q % 2)
                if q:
                    mod_turn(q - 1, 6)
            mod_turn(pairs0[-1], 6)
            pe.wait_ge(sem("mod_ready"), len(pairs0))
            pe.wait_ge(sem("ssm_rows"), 1)
            for m in range(19):
                last = tr(PS[:, 4 + m // 10, (m % 10) * GP:(m % 10) * GP + GP], ssr[:, 16 + m, :], GP)
            last.then_inc(sem("ssm_psum"), 1)
            norms = [0]

            def norm():
                norms[0] += 1
                pe.wait_ge(sem("squares"), norms[0])
                for k in range(KT):
                    last = pe.matmul(PS[:, 7, 0:T], const[:, C_ONE:C_ONE + P], hT[:, k, :],
                                     start=(k == 0), stop=(k == KT - 1))
                last.then_inc(sem("sum_psum"), 1)
                pe.wait_ge(sem("h_ready"), norms[0])

            norm()
            pe.wait_ge(sem("ld_bc"), 96)
            for a in range(2):
                for m in range(2):
                    last = tr(PS[:, 6, (a * 2 + m) * P:(a * 2 + m + 1) * P], x0n[a][:, m, :], P)
            last.then_inc(sem("x0_psum"), 1)
            with pe.Fori(0, 3) as s:
                for h in range(H):
                    pe.wait_ge(sem("hin_credit"), s * H + h + 1)
                    if h % 2 == 0:
                        pe.wait_ge(slab_in[h // 2], s * 16 + (s_hin // RING + 1) * 16)
                    for k in range(KT):
                        last = pe.matmul(PS[:, h % 4, 0:T],
                                         ring[:, h // 2, k * 256 + (h % 2) * P:k * 256 + (h % 2) * P + P],
                                         hT[:, k, :], start=(k == 0), stop=(k == KT - 1))
                        if h % 2 == 0 and k == 0:
                            last.then_inc(slab_credit, 1)
                    last.then_inc(sem("hin_psum"), 1)
            pe.wait_ge(sem("mats_made"), 1)
            g = 0
            for src in (bexp[0], bexp[1], cexp[0], cexp[1]):
                for half in range(2):
                    if g >= 4:
                        pe.wait_ge(sem("mats_turned"), g - 3)
                    for k in range(4):
                        last = tr(PS[:, 4 + g % 4, k * P:(k + 1) * P], src[:, half * 4 + k, :], P)
                    last.then_inc(sem("mats_psum"), 1)
                    g += 1
            g = 3 * H
            for j in range(4):
                arrived(s_hin + 12 + j)
                for i in range(TT):
                    pe.wait_ge(sem("hin_credit"), g + 1)
                    for k in range(KT):
                        last = pe.matmul(PS[0:TOK[i], g % 4, 0:256], hT[:, k, i * P:i * P + TOK[i]],
                                         ring[:, j, k * 256:k * 256 + 256], start=(k == 0), stop=(k == KT - 1))
                        if i == 0 and k == 0:
                            last.then_inc(slab_credit, 1)
                    last.then_inc(sem("hin_psum"), 1)
                    g += 1
            pe.wait_ge(sem("kend_ready"), 1)
            g = 0
            for i in range(TT):
                for half in range(2):
                    if g >= 2:
                        pe.wait_ge(sem("kt_ready"), g - 1)
                    for k in range(4):
                        h = half * 4 + k
                        last = tr(PS[0:TOK[i], 6 + g % 2, k * P:(k + 1) * P], hT[:, h, i * P:i * P + TOK[i]], P)
                    last.then_inc(sem("kt_psum"), 1)
                    g += 1
            pe.wait_ge(sem("kt_ready"), 6)
            for u, (i, L) in enumerate(units):
                n = TOK[i]
                ti = tiles.index(i)
                if L == LEVELS[0]:
                    pe.wait_ge(sem("scores_ready"), ti)
                    for half in range(2):
                        pe.matmul(PS[:, half, :], zero16[:, 0:P], zero16[:], start=True, stop=False, skip_group_check=True)
                if L:
                    b = decayed.index(u)
                    pe.wait_ge(sem("keys_ready"), b + 1)
                if u in masked and masked.index(u):
                    pe.wait_ge(sem("level_read"), masked.index(u))
                for h in range(H):
                    kq = ekq[b % 4][:, h, 0:n] if L else None
                    if u in masked:
                        keys, queries = (kq, kq) if L else (x[:, h, i * P:i * P + n] for x in (hk, hq))
                        at = h * n
                        last = pe.matmul(PS[0:n, 2 + at // 512, at % 512:at % 512 + n], keys, queries, start=True,
                                         stop=True, skip_group_check=True)
                        continue
                    for s0 in range(0, P, 2 * L):
                        c = (h % 4) * P + s0 + L
                        last = pe.matmul(PS[s0:s0 + L, h // 4, c:c + L], kq[:, s0:s0 + L], kq[:, s0 + L:s0 + 2 * L],
                                         start=False, stop=(L == 16 and h % 4 == 3), skip_group_check=True)
                last.then_inc(sem("keys_used"), 1)
                if u in mod_at:
                    mod_rows(mod_at[u], 0, 5)
                    mod_rows(mod_at[u], 1, 5)
                if u in turn_at:
                    mod_turn(turn_at[u], 4)
                if u in sample_at:
                    h = sample_at[u]
                    pe.wait_ge(sem("vmask_ready"), h + 1)
                    if h:
                        pe.wait_ge(sem("state0_new"), h)
                    for half in range(2):
                        last = pe.matmul(PS[:, 6 + half, :], hkt[0:64, 2, h * P:(h + 1) * P],
                                         vmask[0:64, half * 4:half * 4 + 4, :], start=True, stop=True)
                    last.then_inc(sem("state0_psum"), 1)
                if u + 1 != unit_end[i]:
                    continue
                pe.wait_ge(sem("scores_ready"), ti + 1)
                if i == 1:
                    pe.wait_ge(sem("state1_ready"), 1)
                if i == 2:
                    pe.wait_ge(sem("ld_state"), 16)
                    pe.wait_ge(sem("qfull_ready"), 1)
                pe.wait_ge(sem("mod_ready"), turned_by(u))
                for part in range(H * n // 512):
                    op = o_part[i] + part
                    if op:
                        pe.wait_ge(sem("o_read"), op)
                    for h in range(part * 512 // n, (part + 1) * 512 // n):
                        at = (h * n) % 512
                        o = PS[:, 4, at:at + n]
                        last = pe.matmul(o, hv[0:n, i, h * P:(h + 1) * P], scores[0:n, h, 0:n], start=True,
                                         stop=(i == 0), skip_group_check=True)
                        if i == 1:
                            last = pe.matmul(o, st1[:, h, :], hf[:, h, P:2 * P], start=False, stop=True,
                                             skip_group_check=True)
                        if i == 2:
                            for b in range(NB):
                                last = pe.matmul(o[:, b * NS:(b + 1) * NS], st0[:, b, h, :],
                                                 hf[:, h, NP + b * NS:NP + (b + 1) * NS],
                                                 start=False, stop=(b == NB - 1), skip_group_check=True)
                    last.then_inc(sem("o_psum"), 1)
                if i < 2:
                    if i == 0:
                        pe.wait_ge(sem("state0_new"), H)
                    for h in range(H):
                        last = pe.matmul(PS[:, 6 + h // 4, (h % 4) * P:(h % 4 + 1) * P], hkt[:, i, h * P:(h + 1) * P],
                                         hv[:, i, h * P:(h + 1) * P], start=True, stop=True)
                    last.then_inc(sem("state_psum"), 1)
            pe.wait_ge(sem("o_squares"), 1)
            for c in range(5):
                last = pe.matmul(PS[:, c, :], const[:, C_ONE:C_ONE + P], hbflat[:, c * 512:(c + 1) * 512],
                                 start=True, stop=True)
            last.then_inc(sem("o_sums"), 1)
            pe.wait_ge(sem("o_ready"), 1)
            for dt in range(KT):
                n = s_hout + dt // 2
                if dt >= 4:
                    pe.wait_ge(sem("hout_read"), dt - 3)
                if dt % 2 == 0:
                    arrived(n)
                for k in range(KT):
                    last = pe.matmul(PS[:, dt % 4, 0:T], ring[:, n % RING, k * 256 + (dt % 2) * P:k * 256 + (dt % 2) * P + P],
                                     hT[:, k, :], start=(k == 0), stop=(k == KT - 1))
                    if dt % 2 == 0 and k == 0:
                        last.then_inc(slab_credit, 1)
                last.then_inc(sem("hout_psum"), 1)
            norm()

            def gate_up(n, tile, more_tiles, used):
                for sub in range(2):
                    t = tile + sub
                    pe.wait_ge(sem("fin_credit"), t + 1 + more_tiles)
                    for m in range(2):
                        for k in range(KT):
                            last = pe.matmul(PS[:, 2 * (t % 2) + m, 0:T],
                                             ring[:, (n + m) % RING, k * 256 + sub * P:k * 256 + sub * P + P],
                                             hT[:, k, :], start=(k == 0), stop=(k == KT - 1))
                            if sub == 0 and m == 0 and k == 0:
                                last.then_inc(slab_credit, used)
                        last.then_inc(sem("gate_psum" if m == 0 else "up_psum"), 1)

            arrived(s_fin)
            arrived(s_fin + 1)
            gate_up(s_fin, 0, 0, 1)
            with pe.Fori(0, 5) as i:
                for pr in range(2):
                    n = s_fin + 2 + 2 * pr
                    arrived(n, i)
                    arrived(n + 1, i)
                    gate_up(n, 2 + 2 * pr, i * 4, 2)
            pe.wait_ge(sem("mid_ready"), FT)
            with pe.Fori(0, 4) as i:
                for c in range(2):
                    n = s_fout + 2 * c
                    pe.wait_ge(sem("fout_credit"), i * 2 + c + 1)
                    arrived(n, i)
                    arrived(n + 1, i)
                    for k in range(FT):
                        last = pe.matmul(PS[:, c, 0:T], ring[:, (n + k // 11) % RING, (k % 11) * P:(k % 11 + 1) * P],
                                         mid[:, k, :], start=(k == 0), stop=(k == FT - 1))
                        if k == 0:
                            last.then_inc(slab_credit, 2)
                    last.then_inc(sem("fout_psum"), 1)
            norm()
            pe.wait_ge(sem("ld_kept"), 16)

            def states_in(w):
                for j in range(2):
                    gp = 2 * w + j
                    k, q = gp // 4, 32 * (gp % 4)
                    for a in range(2):
                        g = gp * 2 + a
                        if g >= 4:
                            pe.wait_ge(sem("bu_read"), g - 3)
                        pe.matmul(PS[:, g % 4, 0:T], bbt[a][q:q + 32, k, :], hT[q:q + 32, k, :],
                                  start=True, stop=True).then_inc(sem("bu_psum"), 1)

            def states_out(w):
                k = w // 2
                pe.wait_ge(sem("xs_ready"), w + 1)
                if w % 2 == 0 and k >= 2:
                    pe.wait_ge(sem("y5_read"), k - 1)
                for j in range(2):
                    q = 32 * ((2 * w + j) % 4)
                    for a in range(2):
                        last = pe.matmul(PS[q:q + 32, 4 + k % 2, 0:T], cct[a][:, k, q:q + 32],
                                         vb[w % 2][a][:, j, :], start=(a == 0), stop=(a == 1), skip_group_check=True)
                last.then_inc(sem("xs_used"), 1)

            NW = GP // 2
            for w in range(NW):
                states_in(w)
                mod_rows(pairs2[w // 2], w % 2, 6)
                if w:
                    states_out(w - 1)
                if w > 1 and w % 2 == 0:
                    mod_turn(pairs2[w // 2 - 1], 7)
            states_out(NW - 1)
            mod_turn(pairs2[-1], 7)
            pe.wait_ge(sem("mod_ready"), 24)
            pe.wait_ge(sem("fin_states"), NW)
            for a in range(2):
                tr(PS[0:GP, 6, a * P:a * P + P], fin[a][:, 0, :], P)
                for m in range(2):
                    last = tr(PS[:, 7, (a * 2 + m) * P:(a * 2 + m + 1) * P],
                              fin[a][:, 1 + 4 * m:5 + 4 * m, :].rearrange("p b g -> p (b g)"), P)
            last.then_inc(sem("fin_psum"), 1)
            pe.wait_ge(sem("z_ready"), 1)
            with pe.Fori(0, 2) as i:
                for pr in range(2):
                    n = s_glu + 2 * pr
                    arrived(n, i)
                    arrived(n + 1, i)
                    for sub in range(2):
                        pe.wait_ge(sem("glu_credit"), i * 4 + pr * 2 + sub + 1)
                        for m in (1, 0):
                            for k in range(KT):
                                last = pe.matmul(PS[:, 2 * sub + m, 0:T],
                                                 ring[:, (n + m) % RING, k * 256 + sub * P:k * 256 + sub * P + P],
                                                 hT[:, k, :], start=(k == 0), stop=(k == KT - 1))
                                if sub == 0 and m == 1 and k == 0:
                                    last.then_inc(slab_credit, 2)
                            last.then_inc(sem("glu_b_psum" if m else "glu_a_psum"), 1)
            norm()
            pe.sem_inc(sem("expert_credit"), 2)
            pe.wait_ge(sem("ld_router"), 32)
            for i in range(TT):
                n = TOK[i]
                for k in range(KT):
                    pe.matmul(PS[0:n, 4, 16 * i:16 * i + NE], hT[:, k, i * P:i * P + n], wr[:, k, :],
                              start=(k == 0), stop=False)
                last = pe.matmul(PS[0:n, 4, 16 * i:16 * i + NE], const[0:1, C_ONE:C_ONE + n], br[:],
                                 start=False, stop=True)
            last.then_inc(sem("logits"), 1)
            g = 0
            for i in range(TT):
                for half in range(2):
                    if g >= 4:
                        pe.wait_ge(sem("htok_read"), g - 3)
                    for k in range(4):
                        last = tr(PS[0:TOK[i], g % 4, k * P:(k + 1) * P], hT[:, half * 4 + k, i * P:i * P + TOK[i]], P)
                    last.then_inc(sem("htok_psum"), 1)
                    g += 1
            pe.wait_ge(sem("chosen"), 1)
            for i in range(TT):
                n = TOK[i]
                for m in range(i):
                    pe.matmul(PS[0:n, 5, 16 * i:16 * i + NE], const[:, C_ONE:C_ONE + n], rt[:, 2, m, :],
                              start=(m == 0), stop=False)
                pe.matmul(PS[0:n, 5, 16 * i:16 * i + NE], const[0:n, C_BEFORE:C_BEFORE + n], rt[0:n, 2, i, :],
                          start=(i == 0), stop=True)
            for m in range(TT):
                last = pe.matmul(PS[:, 5, 64:64 + NE], const[0:TOK[m], C_ONE:C_ONE + P], rt[0:TOK[m], 2, m, :],
                                 start=(m == 0), stop=(m == TT - 1))
            last.then_inc(sem("places"), 1)
            def gather():
                for half in range(2):
                    for k in range(4):
                        for i in range(TT):
                            kk = half * 4 + k
                            last = pe.matmul(PS[:, 6 + half, k * P:k * P + CAP], htok[0:TOK[i], i, kk * P:(kk + 1) * P],
                                             pick[0:TOK[i], i, :], start=(i == 0), stop=(i == TT - 1))
                            if half == 0 and k == 0 and i == 0:
                                last.then_inc(sem("expert_credit"), 1)
                    last.then_inc(sem("gather_psum"), 1)

            def turn_gates():
                for i in range(TT):
                    last = tr(PS[0:CAP, 3, i * P:i * P + TOK[i]], pickg[0:TOK[i], i, :], TOK[i])
                last.then_inc(sem("pickT_psum"), 1)

            def product(out, a, w, first, end):
                for m, (x, y) in enumerate(((0, 0), (0, 1), (1, 0))):
                    last = pe.matmul(out, a[x], w[y], start=first and m == 0, stop=end and m == 2)
                    if m == 0:
                        begun = last
                return begun, last

            pe.wait_ge(sem("htok_read"), 6)
            pe.wait_ge(sem("pick_ready"), 1)
            gather()
            turn_gates()
            pe.wait_ge(sem("passes_known"), 1)
            n_pass = pe.value_load(npass[0:1, 0:1], min_val=1, max_val=PASSES)
            with pe.Fori(0, n_pass) as ps:
                with pe.Fori(0, NE) as e:
                    it = ps * NE + e

                    def parts(j, lo, hi):
                        return [w[:, j % HRING, lo:hi] for w in wparts]

                    def up(m, s):
                        j = eindex[("gu"[m], s)]
                        pe.wait_ge(sem("rest_ready"), it * NSL + j + 1)
                        for k in range(KT):
                            begun, last = product(PS[0:CAP, s % 2, m * 256:m * 256 + 256],
                                                  [h[:, k, :] for h in hexp], parts(j, k * 256, k * 256 + 256),
                                                  k == 0, k == KT - 1)
                            if k == 0 and j:
                                begun.then_inc(sem("expert_credit"), 1)
                        if m:
                            last.then_inc(sem("eup_psum"), 1)

                    def turn(s):
                        pe.wait_ge(sem("gated_ready"), it * NST + s + 1)
                        if s == 1:
                            pe.wait_ge(sem("pickT_ready"), it + 1)
                        if s >= 2:
                            pe.wait_ge(sem("emid_ready"), it * NST + s - 1)
                        for c in range(2):
                            last = tr(PS[:, 2 + s % 2, c * CAP:(c + 1) * CAP], egated[0:CAP, s % 2, c * P:(c + 1) * P], CAP)
                        last.then_inc(sem("turned_psum"), 1)

                    def down(s):
                        j = eindex[("o", s)]
                        pe.wait_ge(sem("emid_ready"), it * NST + s + 1)
                        pe.wait_ge(sem("rest_ready"), it * NSL + j + 1)
                        for c in range(2):
                            if c:
                                pe.wait_ge(sem("rest2_ready"), it * NST + s + 1)
                            for half in range(2):
                                at = c * D + half * 512
                                begun, last = product(PS[0:CAP, 4 + half, :], [h[:, c * CAP:(c + 1) * CAP] for h in emid[s % 2]],
                                                      parts(j, at, at + 512), s == 0 and c == 0, s == NST - 1 and c == 1)
                                if c == 0 and half == 0:
                                    begun.then_inc(sem("expert_credit"), 1)
                        return last

                    pe.wait_ge(sem("hexp_ready"), it * 2 + 2)
                    pe.wait_ge(sem("scatter_read"), it * KT + KT)
                    for s in range(NST):
                        if s >= 2:
                            pe.wait_ge(sem("gated_ready"), it * NST + s - 1)
                        up(0, s)
                        if s:
                            turn(s - 1)
                        up(1, s)
                        if s >= 2:
                            down(s - 2)
                    turn(NST - 1)
                    down(NST - 2)
                    down(NST - 1).then_inc(sem("y_psum"), 1)
                    pe.wait_ge(sem("pick_ready"), it + 2)
                    gather()
                    pe.wait_ge(sem("yexp_ready"), it + 1)
                    for dt in range(KT):
                        if dt >= 2:
                            pe.wait_ge(sem("scatter_read"), it * KT + KT + dt - 1)
                        pe.matmul(PS[:, dt % 2, 0:T], yexp[0:CAP, dt * P:(dt + 1) * P], pickT[0:CAP, :],
                                  start=True, stop=True).then_inc(sem("scatter_psum"), 1)
                    turn_gates()
            norm()
            g = 0
            for i in range(TT):
                for half in range(2):
                    if g >= 4:
                        pe.wait_ge(sem("y_ready"), g - 3)
                    for k in range(4):
                        last = tr(PS[0:TOK[i], g % 4, k * P:(k + 1) * P], hT[:, half * 4 + k, i * P:i * P + TOK[i]], P)
                    last.then_inc(sem("y_out_psum"), 1)
                    g += 1

        @block.scalar
        def _(act):
            A = nc.scalar.activation
            step = Steps(act, sem("act_step"))
            norms = [0]

            def norm():
                norms[0] += 1
                if norms[0] == 1:
                    act.wait_ge(sem("x_turned"), 6)
                else:
                    act.wait_ge(sem("x_ready"), norms[0] - 1)
                A(hT[:], xT[:], ACT.Square).then_inc(sem("squares"), 1)
                act.wait_ge(sem("sum_psum"), norms[0])
                act.wait_ge(sem("eps_ready"), 1)
                A(root[:], PS[:, 7, 0:T], ACT.Sqrt, bias=epst[:, 0:1], scale=1.0 / D).then_inc(sem("root_ready"), 1)

            act.wait_ge(sem("ld_c"), 32)
            A(crow, crow, ACT.Silu).then_inc(sem("silu_c"), 1)
            act.wait_ge(sem("ld_ssm"), 48)
            A(ssr[:, 2, 2:4], ssr[:, 2, 0:2], ACT.Exp).then_inc(sem("dt_ready"), 1)
            act.wait_ge(sem("angles"), 1)
            A(ssr[:, 32, :], ssr[:, 43, :], ACT.Exp).then_inc(sem("mag_ready"), 1)
            A(ssr[:, 16:32, :], ssr[:, 16:32, :], ACT.Sin).then_inc(sem("sines"), 1)
            def mod_copy(q, bank):
                act.wait_ge(sem("mod_rows_psum"), q + 1)
                if q > 1:
                    act.wait_ge(sem("mod_turn_psum"), q - 1)
                A(modrow[:, q % 2, :], PS[0:NC, bank, :], ACT.Copy).then_inc(sem("mod_rows_read"), 1)

            for q in pairs0:
                mod_copy(q, q % 2)
            norm()
            act.sem_inc(sem("hin_credit"), 4)
            g = 0
            for dst in (hq, hg):
                for h in range(H):
                    act.wait_ge(sem("hin_psum"), g + 1)
                    A(dst[:, h, :], PS[:, g % 4, 0:T], ACT.Silu).then_inc(sem("hin_credit"), 1)
                    g += 1
            for h in range(H):
                act.wait_ge(sem("hin_psum"), g + 1)
                A(hk[:, h, :], PS[:, g % 4, 0:T], ACT.Sigmoid, scale=-1.0)
                A(hb[:, h, :], PS[:, g % 4, 0:T], ACT.Abs)
                A(hf[:, h, :], PS[:, g % 4, 0:T], ACT.Copy).then_inc(sem("hin_credit"), 1)
                g += 1
            for j in range(4):
                for i in range(TT):
                    act.wait_ge(sem("hin_psum"), g + 1)
                    A(hv[0:TOK[i], i, j * 256:j * 256 + 256], PS[0:TOK[i], g % 4, 0:256], ACT.Copy)\
                        .then_inc(sem("hin_credit"), 1)
                    g += 1
            act.wait_ge(sem("prep_stored"), 16)
            act.dma_start(st0.rearrange("p b h e -> p (b h) e"),
                          I["state_hgrn"].rearrange("l b h d e -> d (l b h) e")).then_inc(sem("ld_state"), 16)
            act.wait_ge(sem("hin_credit"), 4 + g)
            step(A(hb, hb, ACT.Exp, scale=-1.0))
            A(hb, hb, ACT.Ln, bias=1.0).then_inc(sem("softplus_ready"), 1)
            act.wait_ge(sem("b_ready"), 1)
            A(hf, hb, ACT.Exp).then_inc(sem("expb_ready"), 1)
            A(decp, hb[:, :, NP - 1], ACT.Exp).then_inc(sem("dec_ready"), 1)
            A(decs, hb[:, :, NP + NS - 1::NS], ACT.Exp).then_inc(sem("dec_ready"), 1)
            a = 0

            def decay(ap):
                nonlocal a
                act.wait_ge(sem("args_ready"), a + 1)
                A(ap, ap, ACT.Exp).then_inc(sem("decays_ready"), 1)
                a += 1

            act.wait_ge(sem("kend_args"), 1)
            A(hT[:], hT[:], ACT.Exp).then_inc(sem("decays_ready"), 1)
            for u, (i, L) in enumerate(units):
                n = TOK[i]
                if L:
                    decay(ekq[decayed.index(u) % 4][:, :, 0:n])
                if u - 1 in mod_at:
                    mod_copy(mod_at[u - 1], 5)
                if u + 1 != unit_end[i]:
                    continue
                for part in range(H * n // 512):
                    op = o_part[i] + part
                    act.wait_ge(sem("o_psum"), op + 1)
                    hs = slice(part * 512 // n, (part + 1) * 512 // n)
                    A(hT[:, hs, i * P:i * P + n], PS[:, 4, :].rearrange("p (h t) -> p h t", t=n), ACT.Copy)\
                        .then_inc(sem("o_read"), 1)
                if i == 0:
                    act.wait_ge(sem("state_psum"), 1)
                    A(st1.rearrange("p (c h) e -> p c (h e)", c=2), PS[:, 6:8, :], ACT.Copy).then_inc(sem("state1_ready"), 1)
            act.wait_ge(sem("o_read"), 5)
            A(hbflat, hT[:].rearrange("p h t -> p (h t)"), ACT.Square).then_inc(sem("o_squares"), 1)
            act.wait_ge(sem("o_sums"), 1)
            A(hk.rearrange("p h t -> p (h t)").rearrange("p (c n) -> p c n", c=5), PS[:, 0:5, :], ACT.Sqrt,
              bias=epst[:, 0:1], scale=1.0 / P).then_inc(sem("o_root"), 1)
            norm()
            with act.Fori(0, FT // 2) as i:
                for c in range(2):
                    act.wait_ge(sem("gate_psum"), i * 2 + c + 1)
                    A(acts[:, c, :], PS[:, 2 * c, 0:T], ACT.Silu).then_inc(sem("silu_ready"), 1)
            norm()
            NW = GP // 2
            for w in range(NW):
                for j in range(2):
                    for a_ in range(2):
                        g = (2 * w + j) * 2 + a_
                        act.wait_ge(sem("bu_psum"), g + 1)
                        if w >= 2:
                            act.wait_ge(sem("v_ready"), w - 1)
                            act.wait_ge(sem("u_used"), w - 1)
                        A(ub[w % 2][a_][:, j, :], PS[:, g % 4, 0:T], ACT.Copy).then_inc(sem("bu_read"), 1)
                if w % 2 == 0 and w:
                    mod_copy(pairs2[w // 2 - 1], 6)
                if w:
                    finals(act, A, w - 1)
            mod_copy(pairs2[-1], 6)
            finals(act, A, NW - 1)
            act.wait_ge(sem("fin_psum"), 1)
            A(fout[0:GP, 0:2, :], PS[0:GP, 6, 0:2 * P].rearrange("p (a n) -> p a n", a=2), ACT.Copy)
            A(fout[:, 2:6, :], PS[:, 7, :].rearrange("p (a n) -> p a n", a=4), ACT.Copy).then_inc(sem("fout_ready"), 1)
            act.wait_ge(sem("y5_read"), KT)
            A(hT[:], hT[:], ACT.Gelu_apprx_tanh).then_inc(sem("z_ready"), 1)
            with act.Fori(0, 4) as i:
                for c in range(2):
                    act.wait_ge(sem("glu_b_psum"), i * 2 + c + 1)
                    A(acts[:, c, :], PS[:, 2 * c + 1, 0:T], ACT.Sigmoid).then_inc(sem("sigmoid_ready"), 1)
            norm()
            g = 0
            for i in range(TT):
                for half in range(2):
                    act.wait_ge(sem("htok_psum"), g + 1)
                    A(htok[0:TOK[i], i, half * 512:half * 512 + 512], PS[0:TOK[i], g % 4, :], ACT.Copy)\
                        .then_inc(sem("htok_read"), 1)
                    g += 1
            act.wait_ge(sem("second_less_first"), 1)
            A(rm[:, 5, :], rm[:, 4, :], ACT.Exp).then_inc(sem("second_exp"), 1)
            def round_slab(it, j):
                act.wait_ge(sem(f"expert_in{eslot(j)}"), it * (uses[eslot(j)] * 16) + arrivals(j) * 16)
                act.wait_ge(sem("expert_credit"), it * NSL + j - HRING + 4)
                A(wparts[0][:, j % HRING, :], eslab(j), ACT.Copy).then_inc(sem("rounded"), 1)

            def gathered(count):
                for half in range(2):
                    act.wait_ge(sem("gather_psum"), count + half)
                    A(hexp[0][:, half * 4:half * 4 + 4, :],
                      PS[:, 6 + half, :].rearrange("p (k n) -> p k n", k=4)[:, :, 0:CAP], ACT.Copy)\
                        .then_inc(sem("hexp_rounded"), 1)

            def gates(count):
                act.wait_ge(sem("pickT_psum"), count)
                A(pickT[0:CAP, :], PS[0:CAP, 3, 0:T], ACT.Copy).then_inc(sem("pickT_ready"), 1)

            round_slab(0, 0)
            round_slab(0, 1)
            gathered(1)
            gates(1)
            act.wait_ge(sem("passes_known"), 1)
            n_pass = act.value_load(npass[0:1, 0:1], min_val=1, max_val=PASSES)
            with act.Fori(0, n_pass) as ps:
                with act.Fori(0, NE) as e:
                    it = ps * NE + e

                    def gate_act(s):
                        act.wait_ge(sem("eup_psum"), it * NST + s + 1)
                        if s >= 2:
                            act.wait_ge(sem("gated_ready"), it * NST + s - 1)
                        A(sig[0:CAP, s % 2, :], PS[0:CAP, s % 2, 0:256], ACT.Silu).then_inc(sem("sig_ready"), 1)

                    def turned(s):
                        act.wait_ge(sem("turned_psum"), it * NST + s + 1)
                        A(emid[s % 2][0], PS[:, 2 + s % 2, 0:2 * CAP], ACT.Copy)\
                            .then_inc(sem("emid_rounded"), 1)

                    for s in range(1, NST):
                        round_slab(it, eindex[("g", s)])
                        gate_act(s - 1)
                        round_slab(it, eindex[("u", s)])
                        if s >= 2:
                            round_slab(it, eindex[("o", s - 2)])
                        turned(s - 1)
                    round_slab(it, NSL - 2)
                    gate_act(NST - 1)
                    round_slab(it, NSL - 1)
                    turned(NST - 1)
                    round_slab(it, NSL)
                    round_slab(it, NSL + 1)
                    act.wait_ge(sem("y_psum"), it + 1)
                    A(yexp[0:CAP, :].rearrange("p (c n) -> p c n", c=2), PS[0:CAP, 4:6, :], ACT.Copy)\
                        .then_inc(sem("yexp_ready"), 1)
                    gathered(it * 2 + 3)
                    gates(it + 2)
            norm()

        @block.vector
        def _(dve):
            V = nc.vector
            step = Steps(dve, sem("dve_step"))

            def tt(out, a, b, op):
                return V.tensor_tensor(out, a, b, op)

            norms = [0]

            def norm(scale_of, shift):
                norms[0] += 1
                n = norms[0]
                if n > 1:
                    dve.wait_ge(sem("h_ready"), n - 1)
                if shift is not None:
                    step(V.scalar_tensor_tensor(scale_a[:], scale_of[1], 1.0, bc(scale_of[0], 2, NC), ALU.add, ALU.mult))
                dve.wait_ge(sem("root_ready"), n)
                step(V.reciprocal(rstd[:], root[:]))
                step(tt(hT[:], xT[:], bc(rstd[:], 1, KT), ALU.mult))
                if shift is None:
                    for k in range(KT):
                        last = V.tensor_scalar(hT[:, k, :], hT[:, k, :], scale_of[0][:, k:k + 1], None, ALU.mult)
                    last.then_inc(sem("h_ready"), 1)
                    return
                s = hT[:, :, NP:].rearrange("p k (b t) -> p k b t", b=NB)
                step(tt(s, s, bc(scale_a[:, :, 1:], 3, NS), ALU.mult))
                V.tensor_tensor(s, s, bc(shift[:, :, 1:], 3, NS), ALU.add)
                for k in range(KT):
                    last = V.tensor_scalar(hT[:, k, 0:NP], hT[:, k, 0:NP], scale_a[:, k, 0:1], shift[:, k, 0:1],
                                           ALU.mult, ALU.add)
                last.then_inc(sem("h_ready"), 1)

            def residual(src, dt, gate, done, sem2=None):
                part = gtmp[:, dt * 64:dt * 64 + 64]
                step(tt(part.rearrange("p (b t) -> p b t", b=NB),
                        src[:, NP:T].rearrange("p (b t) -> p b t", b=NB), bc(gate[:, dt, 1:], 2, NS), ALU.mult))
                V.scalar_tensor_tensor(xT[:, dt, 0:NP], src[:, 0:NP], gate[:, dt, 0:1], xT[:, dt, 0:NP],
                                       ALU.mult, ALU.add)
                last = tt(xT[:, dt, NP:T], xT[:, dt, NP:T], part, ALU.add)
                last.then_inc(done, 1)
                return last

            V.memset(epst[:], EPS).then_inc(sem("eps_ready"), 1)
            V.memset(zero16[:], 0.0).then_inc(sem("zeros"), 1)
            dve.wait_ge(sem("ld_ssm"), 48)
            dve.wait_ge(sem("dt_ready"), 1)
            R = ssr
            two = lambda row: R[:, row, :].rearrange("p (u s) -> p u s", u=2)
            dt_ = bc(R[:, 2, 2:4], 2, 64)
            V.tensor_tensor(two(43), two(0), dt_, ALU.mult)
            step(tt(two(3), two(1), dt_, ALU.mult))
            for k in range(1, 8):
                last = V.tensor_scalar(R[:, 3 + k, :], R[:, 3, :], float(2 ** k), None, ALU.mult)
            step(last)
            an, nn, co, si = R[:, 3:11, :], R[:, 35:43, :], R[:, 16:24, :], R[:, 24:32, :]

            def reduced(out, quarter):
                step(V.tensor_scalar(nn, an, 1.0 / TWO_PI, 0.25 * quarter, ALU.mult, ALU.add))
                step(V.tensor_scalar(nn, nn, ROUND, -ROUND, ALU.add, ALU.add))
                step(V.scalar_tensor_tensor(out, nn, -PI_A, an, ALU.mult, ALU.add))
                step(V.scalar_tensor_tensor(out, nn, -PI_B, out, ALU.mult, ALU.add))
                step(V.scalar_tensor_tensor(out, nn, -PI_C, out, ALU.mult, ALU.add))
                if quarter:
                    step(V.tensor_scalar(out, out, TWO_PI / 4, None, ALU.add))
                return V.tensor_scalar(out, out, 3.1415925, -3.1415925, ALU.min, ALU.max)

            step(reduced(si, 0))
            reduced(co, 1).then_inc(sem("angles"), 1)
            row = lambda r: R[:, r, :]
            dve.wait_ge(sem("mag_ready"), 1)
            dve.wait_ge(sem("sines"), 1)
            step(tt(row(11), row(32), row(16), ALU.mult))
            step(tt(row(12), row(32), row(24), ALU.mult))
            step(V.tensor_scalar(row(11), row(11), -1.0, None, ALU.add))
            step(tt(row(13), row(0), row(0), ALU.mult))
            step(tt(row(14), row(1), row(1), ALU.mult))
            step(tt(row(13), row(13), row(14), ALU.add))
            step(V.reciprocal(row(13), row(13)))
            step(tt(row(14), row(11), row(0), ALU.mult))
            step(tt(row(15), row(12), row(1), ALU.mult))
            step(tt(row(14), row(14), row(15), ALU.add))
            step(tt(row(33), row(14), row(13), ALU.mult))
            step(tt(row(14), row(12), row(0), ALU.mult))
            step(tt(row(15), row(11), row(1), ALU.mult))
            step(tt(row(14), row(14), row(15), ALU.subtract))
            tt(row(34), row(14), row(13), ALU.mult).then_inc(sem("ssm_rows"), 1)
            dve.wait_ge(sem("vecs_psum"), 1)
            step(V.tensor_copy(vecs[:], PS[:, 4, 0:49]))
            step(V.tensor_copy(adab[:], PS[:, 4, 64:160]))
            dve.wait_ge(sem("siluc_psum"), 1)
            V.tensor_copy(siluc[:], PS[:, 5, 0:128].rearrange("p (k c) -> p k c", k=KT)[:, :, 0:NC])\
                .then_inc(sem("siluc_ready"), 1)
            g = 0
            for i in range(TT):
                for half in range(2):
                    dve.wait_ge(sem("x_psum"), g + 1)
                    V.tensor_copy(xT[:, half * 4:half * 4 + 4, i * P:i * P + TOK[i]],
                                  PS[:, 2 * (i % 2) + half, :].rearrange("p (k t) -> p k t", k=4)[:, :, 0:TOK[i]])\
                        .then_inc(sem("x_turned"), 1)
                    g += 1
            def mod_bias(q, bank):
                dve.wait_ge(sem("mod_turn_psum"), q + 1)
                tt(mod[:, 4 * q:4 * q + 4, :], PS[:, bank, 0:4 * NC].rearrange("p (a c) -> p a c", a=4),
                   bc(adab[:, 4 * q:4 * q + 4], 2, NC), ALU.add).then_inc(sem("mod_ready"), 1)

            for q in pairs0:
                mod_bias(q, 6)
            dve.wait_ge(sem("ssm_psum"), 1)
            V.tensor_copy(sT[:, 0:10, :], PS[:, 4, 0:320].rearrange("p (m g) -> p m g", g=GP))
            step(V.tensor_copy(sT[:, 10:19, :], PS[:, 5, 0:288].rearrange("p (m g) -> p m g", g=GP)))
            dve.wait_ge(sem("mod_ready"), 4)
            norm((vecs[:, 0:8], layer_mod(0, 1)), layer_mod(0, 0))
            dve.wait_ge(sem("x0_psum"), 1)
            for a in range(2):
                last = V.tensor_copy(x0T[a].rearrange("p b g -> p (b g)"), PS[:, 6, a * 256:a * 256 + 256])
            step(last)
            for a in range(2):
                last = tt(lamT[a], sT[:, 16, :], sT[:, 8 * a, :], ALU.mult)
            step(last)
            lr, li = (bc(lamT[a], 1, NB) for a in range(2))
            step(tt(addT[0], x0T[0], lr, ALU.mult))
            step(tt(addT[1], x0T[1], li, ALU.mult))
            step(tt(addT[0], addT[0], addT[1], ALU.subtract))
            step(tt(x0T[1], x0T[1], lr, ALU.mult))
            step(tt(addT[1], x0T[0], li, ALU.mult))
            step(tt(addT[1], addT[1], x0T[1], ALU.add))
            dve.wait_ge(sem("ld_bc"), 96)
            cr, ci = (bc(sT[:, 17 + a, :], 2, 16) for a in range(2))
            dve.wait_ge(sem("bexp_zero"), 2)
            for a, (f, g2, op) in enumerate(((0, 1, ALU.subtract), (1, 0, ALU.add))):
                step(tt(t512[0], bnat[f], cr, ALU.mult))
                step(tt(t512[1], bnat[g2], ci, ALU.mult))
                for half in range(2):
                    p0 = 64 * half
                    o = bexp[a].rearrange("p k (j u c) -> p (k j) u c", j=4, u=2)[p0:p0 + 64, :, half, :]
                    last = tt(o, t512[0][p0:p0 + 64], t512[1][p0:p0 + 64], op)
                step(last)
            for a in range(2):
                for u in range(2):
                    last = V.tensor_scalar(cexp[a][:, :, 64 * u:64 * u + 64], cnat[a], const[:, C_PAR + u:C_PAR + u + 1],
                                           -1.0 if a else 1.0, ALU.mult, ALU.mult)
            last.then_inc(sem("mats_made"), 1)
            g = 0
            for dst in (bbt[0], bbt[1], cct[0], cct[1]):
                for half in range(2):
                    dve.wait_ge(sem("mats_psum"), g + 1)
                    V.tensor_copy(dst[:, half * 4:half * 4 + 4, :],
                                  PS[:, 4 + g % 4, :].rearrange("p (k n) -> p k n", k=4))\
                        .then_inc(sem("mats_turned"), 1)
                    g += 1
            dve.wait_ge(sem("softplus_ready"), 1)
            step(V.scalar_tensor_tensor(hf, hf, 0.0, hb, ALU.min, ALU.subtract))
            for h in range(H):
                last = V.tensor_tensor_scan(hb[:, h, :], const[:, C_KEEP:C_KEEP + T], hf[:, h, :], 0.0, ALU.mult, ALU.add)
            last.then_inc(sem("b_ready"), 1)
            dve.wait_ge(sem("b_ready"), 1)
            for i in range(2):
                tt(hT[:, :, i * P:i * P + P], bc(hb[:, :, i * P + P - 1], 2, P), hb[:, :, i * P:i * P + P], ALU.subtract)
            sv = lambda ap: ap[:, :, NP:T].rearrange("p h (b t) -> p h b t", b=NB)
            tt(sv(hT[:]), bc(sv(hb)[:, :, :, NS - 1], 3, NS), sv(hb), ALU.subtract).then_inc(sem("kend_args"), 1)
            dve.wait_ge(sem("expb_ready"), 1)
            tt(hf, hf, hq, ALU.mult).then_inc(sem("qfull_ready"), 1)
            a = 1
            dve.wait_ge(sem("decays_ready"), a)
            tt(hT[:], hT[:], hk, ALU.mult).then_inc(sem("kend_ready"), 1)
            g = 0
            for i in range(TT):
                for half in range(2):
                    dve.wait_ge(sem("kt_psum"), g + 1)
                    V.tensor_copy(hkt[0:TOK[i], i, half * 512:half * 512 + 512], PS[0:TOK[i], 6 + g % 2, :])\
                        .then_inc(sem("kt_ready"), 1)
                    g += 1
            dve.wait_ge(sem("ld_masks"), 16)

            def add_level(u):
                i, L = units[u]
                n = TOK[i]
                dve.wait_ge(sem("keys_used"), u + 1)
                src = PS[0:n, 2:2 + H * n // 512, :].rearrange("p c x -> p (c x)").rearrange("p (h t) -> p h t", h=H)
                mask = bc(const[0:n, C_ID:C_ID + n] if L == 0 else lmask[0:n, LEVELS.index(L) - 3, 0:n], 1, H)
                first = not units[u - 1][0] == i or u - 1 not in masked if u else True
                out = scores[0:n, :, 0:n] if first else hT[0:n, :, i * P:i * P + n]
                if first and i != 2:
                    dve.wait_ge(sem("o_psum"), o_part[i])
                tt(out, src, mask, ALU.mult).then_inc(sem("level_read"), 1)
                dve.wait_ge(sem("level_read"), masked.index(u) + 1)
                if not first:
                    return tt(scores[0:n, :, 0:n], scores[0:n, :, 0:n], out, ALU.add)

            for u, (i, L) in enumerate(units):
                n = TOK[i]
                if L:
                    a += 1
                    dve.wait_ge(sem("decays_ready"), a)
                    halves = lambda ap: ap.rearrange("p h (b w) -> p h b w", w=2 * L)
                    e, k, q = (halves(x) for x in (ekq[decayed.index(u) % 4][:, :, 0:n], hk[:, :, i * P:i * P + n],
                                                   hq[:, :, i * P:i * P + n]))
                    tt(e[:, :, :, 0:L], e[:, :, :, 0:L], k[:, :, :, 0:L], ALU.mult)
                    tt(e[:, :, :, L:], e[:, :, :, L:], q[:, :, :, L:], ALU.mult).then_inc(sem("keys_ready"), 1)
                if u - 1 in turn_at:
                    mod_bias(turn_at[u - 1], 4)
                if u - 1 in masked and u != unit_end.get(units[u - 1][0]):
                    add = add_level(u - 1)
                    if add:
                        step(add)
                if u in sample_at:
                    h = sample_at[u]
                    sl = st0[:, :, h, :]
                    if h == 0:
                        dve.wait_ge(sem("o_psum"), 1)
                        dve.wait_ge(sem("dec_ready"), 2)
                    step(tt(sl, sl, bc(decs[:, h, :], 2, P), ALU.mult))
                    dve.wait_ge(sem("state0_psum"), 1 + h)
                    tt(sl, sl, PS[:, 6:8, :].rearrange("p c (b e) -> p (c b) e", b=4), ALU.add).then_inc(sem("state0_new"), 1)
                if u + 1 != unit_end[i]:
                    continue
                if i == 2:
                    add_level(u).then_inc(sem("scores_ready"), 1)
                else:
                    step(add_level(u))
                    tt(scores[:, :, :].rearrange("p (c h) t -> p c (h t)", c=2), scores[:, :, :].rearrange("p (c h) t -> p c (h t)", c=2),
                       PS[:, 0:2, :], ALU.add).then_inc(sem("scores_ready"), 1)
                if i == 1:
                    dve.wait_ge(sem("state_psum"), 2)
                    for h in range(H):
                        last = V.scalar_tensor_tensor(st1[:, h, :], st1[:, h, :], decp[:, h:h + 1],
                                                      PS[:, 6 + h // 4, (h % 4) * P:(h % 4 + 1) * P], ALU.mult, ALU.add)
                    last.then_inc(sem("state1_ready"), 1)
            dve.wait_ge(sem("o_root"), 1)
            step(V.reciprocal(hk, hk))
            step(tt(hT[:], hT[:], hk, ALU.mult))
            V.scalar_tensor_tensor(hT[:], hT[:], vecs[:, 48:49], hg, ALU.mult, ALU.mult).then_inc(sem("o_ready"), 1)
            for dt in range(KT):
                dve.wait_ge(sem("hout_psum"), dt + 1)
                residual(PS[:, dt % 4, :], dt, layer_mod(0, 2), sem("hout_read"))
            dve.wait_ge(sem("hout_read"), KT)
            dve.sem_inc(sem("x_ready"), 1)
            norm((vecs[:, 8:16], layer_mod(0, 4)), layer_mod(0, 3))
            dve.sem_inc(sem("fin_credit"), 2)
            with dve.Fori(0, FT // 2) as i:
                for c in range(2):
                    dve.wait_ge(sem("up_psum"), i * 2 + c + 1)
                    dve.wait_ge(sem("silu_ready"), i * 2 + c + 1)
                    tt(midf[:, bass.ds(i * (2 * T) + c * T, T)], acts[:, c, :], PS[:, 2 * c + 1, 0:T], ALU.mult)\
                        .then_inc(sem("fin_credit"), 1)
            dve.wait_ge(sem("fin_credit"), 2 + FT)
            dve.sem_inc(sem("mid_ready"), FT)
            dve.sem_inc(sem("fout_credit"), 2)
            for dt in range(KT):
                dve.wait_ge(sem("fout_psum"), dt + 1)
                residual(PS[:, dt % 2, :], dt, layer_mod(0, 5), sem("fout_credit"))
            dve.wait_ge(sem("fout_credit"), 2 + KT)
            dve.sem_inc(sem("x_ready"), 1)
            norm((vecs[:, 16:24], layer_mod(1, 1)), layer_mod(1, 0))
            dve.wait_ge(sem("tables_ready"), 1)
            NW = GP // 2
            for w in range(NW):
                v, z, u = vb[w % 2], zb, ub[w % 2]
                dve.wait_ge(sem("bu_read"), 4 * w + 4)
                if w >= 2:
                    dve.wait_ge(sem("xs_used"), w - 1)
                    dve.wait_ge(sem("fin_states"), w - 1)
                for a in range(2):
                    first = u[a][:, :, NP::NS]
                    last = tt(first, first, addT[a][:, :, 2 * w:2 * w + 2].rearrange("p b g -> p g b"), ALU.add)
                step(last)
                rotate(step, tt, v, u, wd, w, ALU.add, ALU.subtract, (1,))
                dve.sem_inc(sem("u_used"), 1)
                dve.wait_ge(sem("v_ready"), w + 1)
                for j in range(2):
                    gp = 2 * w + j
                    for b in range(2):
                        V.tensor_tensor_scan(z[b][:, j, 0:NP], sT[:, 16, gp:gp + 1].to_broadcast([P, NP]), v[b][:, j, 0:NP],
                                             0.0, ALU.mult, ALU.add)
                        last = V.tensor_tensor_scan(z[b][:, j, NP:T], magk[:, gp, :], v[b][:, j, NP:T], 0.0, ALU.mult, ALU.add)
                step(last)
                rotate(step, tt, v, z, wd, w, ALU.subtract, ALU.add)
                dve.sem_inc(sem("xs_ready"), 1)
                if w > 2 and w % 2:
                    mod_bias(pairs2[w // 2 - 1], 7)
                if w % 2 == 1 and w > 2:
                    k = w // 2 - 1
                    dve.wait_ge(sem("xs_used"), w - 1)
                    V.scalar_tensor_tensor(hT[:, k, :], hT[:, k, :], vecs[:, 40 + k:41 + k], PS[:, 4 + k % 2, 0:T],
                                           ALU.mult, ALU.add).then_inc(sem("y5_read"), 1)
            mod_bias(pairs2[-1], 7)
            k = KT - 1
            dve.wait_ge(sem("xs_used"), NW)
            V.scalar_tensor_tensor(hT[:, k, :], hT[:, k, :], vecs[:, 40 + k:41 + k], PS[:, 4 + k % 2, 0:T],
                                   ALU.mult, ALU.add).then_inc(sem("y5_read"), 1)
            dve.sem_inc(sem("glu_credit"), 2)
            for dt in range(KT):
                dve.wait_ge(sem("glu_a_psum"), dt + 1)
                dve.wait_ge(sem("sigmoid_ready"), dt + 1)
                if dt:
                    dve.wait_ge(sem("glu_credit"), 2 + dt)
                step(tt(gated[:], acts[:, dt % 2, :], PS[:, 2 * (dt % 2), 0:T], ALU.mult))
                residual(gated[:], dt, layer_mod(1, 2), sem("glu_credit"))
            dve.wait_ge(sem("glu_credit"), 2 + KT)
            dve.sem_inc(sem("x_ready"), 1)
            norm((vecs[:, 24:32], layer_mod(1, 4)), layer_mod(1, 3))
            dve.wait_ge(sem("s5_out"), 64)
            step(V.memset(rt, 0.0))
            step(V.memset(macc, 0.0))
            L, one, chosen, gate, place, l2, t1, t2, two_ = (rt[:, r] for r in range(9))
            dve.wait_ge(sem("logits"), 1)
            for i in range(TT):
                last = V.tensor_copy(L[0:TOK[i], i, :], PS[0:TOK[i], 4, 16 * i:16 * i + NE])
            step(last)
            step(V.tensor_scalar(rt[:, 9, 0, :], const[:, C_IOTA:C_IOTA + NE], -1.0, float(NE), ALU.mult, ALU.add))
            rank = bc(rt[:, 9, 0, :], 1, TT)

            def best(out, lg, m, mm):
                step(V.tensor_reduce(rm[:, m, :], lg, AX.X, ALU.max))
                step(tt(t1, lg, bc(rm[:, m, :], 2, NE), ALU.is_equal))
                step(tt(t1, t1, rank, ALU.mult))
                step(V.tensor_reduce(rm[:, mm, :], t1, AX.X, ALU.max))
                step(tt(out, t1, bc(rm[:, mm, :], 2, NE), ALU.is_equal))

            best(one, L, 0, 1)
            step(V.scalar_tensor_tensor(l2, one, -3.0e38, L, ALU.mult, ALU.add))
            best(two_, l2, 2, 3)
            tt(chosen, one, two_, ALU.add).then_inc(sem("chosen"), 1)
            dve.wait_ge(sem("chosen"), 1)
            tt(rm[:, 4, :], rm[:, 2, :], rm[:, 0, :], ALU.subtract).then_inc(sem("second_less_first"), 1)
            dve.wait_ge(sem("second_exp"), 1)
            step(V.tensor_scalar(rm[:, 6, :], rm[:, 5, :], 1.0, None, ALU.add))
            step(V.reciprocal(rm[:, 6, :], rm[:, 6, :]))
            step(tt(rm[:, 7, :], rm[:, 6, :], rm[:, 5, :], ALU.mult))
            step(tt(t1, one, bc(rm[:, 6, :], 2, NE), ALU.mult))
            step(tt(t2, two_, bc(rm[:, 7, :], 2, NE), ALU.mult))
            step(tt(gate, t1, t2, ALU.add))
            dve.wait_ge(sem("places"), 1)
            for i in range(TT):
                last = V.tensor_copy(place[0:TOK[i], i, :], PS[0:TOK[i], 5, 16 * i:16 * i + NE])
            step(last)
            step(V.scalar_tensor_tensor(place, place, 1.0, chosen, ALU.add, ALU.mult))
            step(V.tensor_scalar(place, place, -1.0, None, ALU.add))
            cnt = rt[0:1, 10, 0, 0:1]
            step(V.tensor_reduce(cnt, PS[0:1, 5, 64:64 + NE], AX.X, ALU.max))
            step(V.tensor_scalar(rt[0:1, 11, 0, 0:1], cnt, float(CAP), None, ALU.is_gt))
            for k in range(2, PASSES):
                step(V.scalar_tensor_tensor(rt[0:1, 11, 0, 0:1], cnt, float(CAP * k), rt[0:1, 11, 0, 0:1], ALU.is_gt, ALU.add))
            V.tensor_scalar(npass[:], rt[0:1, 11, 0, 0:1], 1.0, None, ALU.add).then_inc(sem("passes_known"), 1)
            dve.wait_ge(sem("passes_known"), 1)
            V.tensor_copy(xplace[:, 0:NE, :], place.rearrange("p i e -> p e i"))
            V.tensor_copy(xgate[:, 0:NE, :], gate.rearrange("p i e -> p e i"))
            V.tensor_copy(xgate[:, NE, :], gate[:, :, 0])
            step(V.tensor_scalar(xplace[:, NE, :], place[:, :, 0], -float(CAP), None, ALU.add))
            xplacef = xplace.rearrange("p e i -> p (e i)")
            xgatef = xgate.rearrange("p e i -> p (e i)")

            def pick_tokens(e):
                for i in range(TT):
                    n = TOK[i]
                    at = bass.ds(e * TT + i, 1)
                    V.tensor_scalar(pick[0:n, i, :], const[0:n, C_IOTA:C_IOTA + CAP], xplacef[0:n, at], None, ALU.is_equal)
                    last = V.tensor_scalar(pickg[0:n, i, :], const[0:n, C_IOTA:C_IOTA + CAP], xplacef[0:n, at],
                                           xgatef[0:n, at], ALU.is_equal, ALU.mult)
                last.then_inc(sem("pick_ready"), 1)

            def rest_slab(it, j):
                dve.wait_ge(sem("rounded"), it * NSL + j + 1)
                n = D if order[j % NSL][0] == "o" else SLAB
                tt(wparts[1][:, j % HRING, 0:n], eslab(j)[:, 0:n], f32(wparts[0][:, j % HRING, 0:n]), ALU.subtract)\
                    .then_inc(sem("rest_ready"), 1)

            def gathered(count):
                for half in range(2):
                    dve.wait_ge(sem("hexp_rounded"), count + half)
                    hs = slice(half * 4, half * 4 + 4)
                    tt(hexp[1][:, hs, :], PS[:, 6 + half, :].rearrange("p (k n) -> p k n", k=4)[:, :, 0:CAP],
                       f32(hexp[0][:, hs, :]), ALU.subtract).then_inc(sem("hexp_ready"), 1)

            pick_tokens(0)
            rest_slab(0, 0)
            gathered(1)
            rest_slab(0, 1)
            dve.sem_inc(sem("scatter_read"), KT)
            dve.sem_inc(sem("place_moved"), 1)
            n_pass = dve.value_load(npass[0:1, 0:1], min_val=1, max_val=PASSES)
            with dve.Fori(0, n_pass) as ps:
                with dve.Fori(0, NE) as e:
                    it = ps * NE + e

                    def gate_mul(s):
                        dve.wait_ge(sem("sig_ready"), it * NST + s + 1)
                        if s >= 2:
                            dve.wait_ge(sem("turned_psum"), it * NST + s - 1)
                        tt(egated[0:CAP, s % 2, :], sig[0:CAP, s % 2, :], PS[0:CAP, s % 2, 256:512], ALU.mult)\
                            .then_inc(sem("gated_ready"), 1)

                    def turned(s):
                        dve.wait_ge(sem("emid_rounded"), it * NST + s + 1)
                        rounded, rest = emid[s % 2]
                        tt(rest, PS[:, 2 + s % 2, 0:2 * CAP], f32(rounded), ALU.subtract).then_inc(sem("emid_ready"), 1)

                    for s in range(1, NST):
                        rest_slab(it, eindex[("g", s)])
                        gate_mul(s - 1)
                        rest_slab(it, eindex[("u", s)])
                        if s >= 2:
                            rest_slab(it, eindex[("o", s - 2)])
                        turned(s - 1)
                    rest_slab(it, NSL - 2)
                    gate_mul(NST - 1)
                    rest_slab(it, NSL - 1)
                    turned(NST - 1)
                    dve.wait_ge(sem("place_moved"), it + 1)
                    pick_tokens(e + 1)
                    dve.wait_ge(sem("pick_ready"), it + 2)
                    at = bass.ds((e + 1) * TT, TT)
                    V.tensor_scalar(xplacef[:, at], xplacef[:, at], -float(CAP), None, ALU.add).then_inc(sem("place_moved"), 1)
                    rest_slab(it, NSL)
                    rest_slab(it, NSL + 1)
                    gathered(it * 2 + 3)
                    for dt in range(KT):
                        dve.wait_ge(sem("scatter_psum"), it * KT + dt + 1)
                        tt(macc[:, dt, :], macc[:, dt, :], PS[:, dt % 2, 0:T], ALU.add).then_inc(sem("scatter_read"), 1)
                    dve.wait_ge(sem("scatter_read"), it * KT + 2 * KT)
            for dt in range(KT):
                last = residual(macc[:, dt, :], dt, layer_mod(1, 5), sem("x_macc"))
            dve.wait_ge(sem("x_macc"), KT)
            dve.sem_inc(sem("x_ready"), 1)
            norm((vecs[:, 32:40], None), None)
            g = 0
            for i in range(TT):
                for half in range(2):
                    dve.wait_ge(sem("y_out_psum"), g + 1)
                    V.tensor_copy(yout[0:TOK[i], i, half * 512:half * 512 + 512], PS[0:TOK[i], g % 4, :])\
                        .then_inc(sem("y_ready"), 1)
                    g += 1

        @block.gpsimd
        def _(pool):
            G = nc.gpsimd
            step = Steps(pool, sem("pool_step"))

            def tt(out, a, b, op):
                return G.tensor_tensor(out, a, b, op)

            for a in range(2):
                G.memset(bexp[a], 0.0).then_inc(sem("bexp_zero"), 1)
            pool.wait_ge(sem("mats_turned"), 8)
            pool.dma_start(prep, kept).then_inc(sem("prep_stored"), 16)
            pool.wait_ge(sem("b_ready"), 1)
            pool.wait_ge(sem("zeros"), 1)
            for u, (i, L) in enumerate(units):
                n = TOK[i]
                if L:
                    b = decayed.index(u)
                    if b >= 4:
                        pool.wait_ge(sem("keys_used"), decayed[b - 4] + 1)
                    e, x = (ap.rearrange("p h (b w) -> p h b w", w=2 * L) for ap in
                            (ekq[b % 4][:, :, 0:n], hb[:, :, i * P:i * P + n]))
                    middle = bc(x[:, :, :, L - 1], 3, L)
                    tt(e[:, :, :, 0:L], middle, x[:, :, :, 0:L], ALU.subtract)
                    tt(e[:, :, :, L:], x[:, :, :, L:], middle, ALU.subtract).then_inc(sem("args_ready"), 1)
                if u in sample_at:
                    h = sample_at[u]
                    if h:
                        pool.wait_ge(sem("state0_psum"), h)
                    tt(vmask[0:64], bc(hv[0:64, 2, h * P:(h + 1) * P], 1, NB), bc(const[0:64, C_SAMPLE:C_SAMPLE + NB], 2, P),
                       ALU.mult).then_inc(sem("vmask_ready"), 1)
            pool.wait_ge(sem("hgrn_out"), 32)
            pool.wait_ge(sem("o_ready"), 1)
            tt(magk, bc(sT[:, 16, :], 2, NB * NS), bc(const[:, C_KEEP + NP:C_KEEP + T], 1, GP), ALU.mult)
            G.memset(rot_c[:, :, 0:1], 1.0)
            step(G.memset(rot_s[:, :, 0:1], 0.0))
            for k in range(8):
                n = 2 ** k
                for c in range(0, n, 32):
                    m = min(n, 32)
                    pc, psn = bc(sT[:, k, :], 2, m), bc(sT[:, 8 + k, :], 2, m)
                    c0, s0 = rot_c[:, :, c:c + m], rot_s[:, :, c:c + m]
                    c1, s1 = rot_c[:, :, n + c:n + c + m], rot_s[:, :, n + c:n + c + m]
                    ta, tb = rtmp[0][:, :, 0:m], rtmp[1][:, :, 0:m]
                    step(tt(c1, c0, pc, ALU.mult))
                    step(tt(ta, s0, psn, ALU.mult))
                    step(tt(s1, c0, psn, ALU.mult))
                    step(tt(tb, s0, pc, ALU.mult))
                    step(tt(c1, c1, ta, ALU.subtract))
                    step(tt(s1, s1, tb, ALU.add))
            pool.sem_inc(sem("tables_ready"), 1)
            pool.wait_ge(sem("ld_kept"), 16)
            NW = GP // 2
            for w in range(NW):
                u = ub[w % 2]
                pool.wait_ge(sem("bu_read"), 4 * w + 4)
                if w >= 2:
                    pool.wait_ge(sem("xs_used"), w - 1)
                    pool.wait_ge(sem("fin_states"), w - 1)
                rotate(step, tt, vb[w % 2], u, wp, w, ALU.add, ALU.subtract, (0,))
                pool.sem_inc(sem("v_ready"), 1)
            pool.wait_ge(sem("passes_known"), 1)
            n_pass = pool.value_load(npass[0:1, 0:1], min_val=1, max_val=PASSES)
            with pool.Fori(0, n_pass) as ps:
                with pool.Fori(0, NE) as e:
                    it = ps * NE + e
                    for s in range(NST):
                        j = eindex[("o", s)]
                        pool.wait_ge(sem("rounded"), it * NSL + j + 1)
                        tt(wparts[1][:, j % HRING, D:2 * D], eslab(j)[:, D:2 * D], f32(wparts[0][:, j % HRING, D:2 * D]),
                           ALU.subtract)\
                            .then_inc(sem("rest2_ready"), 1)


def constants(np):
    c = np.zeros((P, C_W), np.float32)
    s = np.arange(P)[:, None]
    t = np.arange(P)[None, :]
    c[:, C_ID:C_ID + P] = s == t
    c[:, C_BEFORE:C_BEFORE + P] = s < t
    c[:, C_ONE:C_ONE + P] = 1
    c[:, C_SAMPLE:C_SAMPLE + NB] = s // NS == t[:, 0:NB]
    keep = np.ones(T, np.float32)
    keep[[0, P]] = 0
    keep[NP::NS] = 0
    c[:, C_KEEP:C_KEEP + T] = keep
    c[:, C_PAR:C_PAR + 2] = (s // 16) % 2 == t[:, 0:2]
    c[:, C_IOTA:C_IOTA + P] = t
    return c


def level_masks(np):
    s, t = np.arange(P)[:, None], np.arange(P)[None, :]
    return np.concatenate([(s // (2 * L) == t // (2 * L)) & (s % (2 * L) < L) & (t % (2 * L) >= L)
                           for L in LEVELS[3:-1]], axis=1).astype(np.float32)


_INS = ["x_prompt", "x_sample", "state_hgrn", "state_ssm_re", "state_ssm_im", "c_prompt", "c_sample", "norm_w",
        "ada_w", "ada_b", "hgrn_w_in", "hgrn_gnorm", "hgrn_w_out", "ssm_a_re", "ssm_a_im",
        "ssm_log_dt", "ssm_b_re", "ssm_b_im", "ssm_c_re", "ssm_c_im", "ssm_d", "ssm_w_glu", "ffn_w_in", "ffn_w_out",
        "moe_w_router", "moe_b_router", "moe_w_in", "moe_w_out", "final_norm_w"]
_OUTS = [(1, NP, D), (NB, NS, D), (1, 1, H, P, P), (1, 1, 64, 64), (1, 1, 64, 64), (1, NB, H, P, P), (1, NB, 64, 64),
         (1, NB, 64, 64)]


def kernel(**inputs):
    import numpy as np
    from concourse import bacc
    from concourse.bass_utils import run_bass_kernel_spmd

    nc = bacc.Bacc("TRN2", target_bir_lowering=False, num_devices=1)
    arrays, ins = {}, {}
    for name in _INS:
        arrays[f"in_{name}"] = np.ascontiguousarray(inputs[name])
    arrays["in_constants"] = constants(np)
    arrays["in_level_masks"] = level_masks(np)
    for name in [*_INS, "constants", "level_masks"]:
        ins[name] = nc.dram_tensor(f"in_{name}", arrays[f"in_{name}"].shape, F32, kind="ExternalInput").ap()
    outs = [nc.dram_tensor(f"out_{i}", shape, F32, kind="ExternalOutput").ap() for i, shape in enumerate(_OUTS)]
    prep = nc.dram_tensor("s5_prep", (P, 5120), F32).ap()
    trunk(nc, ins, outs, prep)
    r = run_bass_kernel_spmd(nc, [arrays], core_ids=[0])
    return tuple(r.results[0][f"out_{i}"] for i in range(len(_OUTS)))
```
